# Optimizing a Trainium2 kernel written in Bass

```python
import math
import jax, jax.numpy as jnp
from jax import lax
import numpy as np
import functools

D_MODEL = 1024
BATCH = 1
SEQ = 256
DEPTH = 1

CONV_CH = D_MODEL // 2
CONV_WIDTH = 31
DA_HEADS = 4
DA_HEAD_DIM = 64
DA_V_DIM = 2 * DA_HEAD_DIM
ATTN_W = DA_HEADS * DA_V_DIM
N_BRANCH = 2
COL_CONV = 2 * CONV_CH
COL_Q = DA_HEADS * 2 * DA_HEAD_DIM
COL_K = DA_HEADS * 2 * DA_HEAD_DIM
COL_V = ATTN_W
COL_GATE = N_BRANCH * D_MODEL
IN_COLS = COL_CONV + COL_Q + COL_K + COL_V + COL_GATE
N_GROUPS = 4
EXPERTS_PER_GROUP = 8
N_EXPERTS = N_GROUPS * EXPERTS_PER_GROUP
TOP_K_IN_GROUP = 2
D_EXPERT = D_MODEL // 2

Q_BLOCK = 128
ROW_BLOCK = 128
EPS = 1e-6


def rms_norm(x, g):
    xf = x.astype(jnp.float32)
    y = xf * lax.rsqrt(jnp.mean(xf * xf, axis=-1, keepdims=True) + EPS)
    return (y * g.astype(jnp.float32)).astype(x.dtype)

def layer_norm(x, g, b):
    xf = x.astype(jnp.float32)
    mu = jnp.mean(xf, axis=-1, keepdims=True)
    var = jnp.mean(jnp.square(xf - mu), axis=-1, keepdims=True)
    y = (xf - mu) * lax.rsqrt(var + EPS)
    return (y * g.astype(jnp.float32) + b.astype(jnp.float32)).astype(x.dtype)

def conformer_conv(u, dw_w, dw_b, ln_g, ln_b):
    a, gate = jnp.split(u, 2, axis=-1)
    y = a * jax.nn.sigmoid(gate)
    y = lax.conv_general_dilated(
        y, dw_w[:, None, :].astype(y.dtype), window_strides=(1,),
        padding=[(CONV_WIDTH - 1, 0)],
        dimension_numbers=("NWC", "WIO", "NWC"),
        feature_group_count=CONV_CH) + dw_b
    y = layer_norm(y, ln_g, ln_b)
    return jax.nn.silu(y)

def diff_attention(q, k, v, lam, subln_g, lam_init):
    B, S = q.shape[0], q.shape[1]
    nb = S // Q_BLOCK
    scale = DA_HEAD_DIM ** -0.5
    qb = q.reshape(B, nb, Q_BLOCK, DA_HEADS, 2, DA_HEAD_DIM).transpose(1, 0, 2, 3, 4, 5)
    key_pos = jnp.arange(S)

    def block(args):
        qi, bi = args
        s = jnp.einsum("bqhcd,bkhcd->bhcqk", qi, k,
                       preferred_element_type=jnp.float32) * scale
        q_pos = bi * Q_BLOCK + jnp.arange(Q_BLOCK)
        mask = key_pos[None, :] <= q_pos[:, None]
        s = jnp.where(mask, s, -jnp.inf)
        p = jax.nn.softmax(s, axis=-1)
        a = (p[:, :, 0] - lam * p[:, :, 1]).astype(v.dtype)
        return jnp.einsum("bhqk,bkhe->bqhe", a, v)

    o = lax.map(block, (qb, jnp.arange(nb)))
    o = o.transpose(1, 0, 2, 3, 4).reshape(B, S, DA_HEADS, DA_V_DIM)
    o = rms_norm(o, subln_g) * (1.0 - lam_init)
    return o.reshape(B, S, ATTN_W)

def hierarchical_moe(h, w_rg, b_rg, w_re, b_re, w_g, w_u, w_d):
    B, S, D = h.shape
    T = B * S
    hf = h.reshape(T, D)
    g_logits = jnp.matmul(hf, w_rg, preferred_element_type=jnp.float32) + b_rg.astype(jnp.float32)
    g_prob = jax.nn.softmax(g_logits, axis=-1)
    g_sel = jnp.argmax(g_logits, axis=-1)
    g_w = jnp.take_along_axis(g_prob, g_sel[:, None], axis=1)
    e_logits = (jnp.matmul(hf, w_re, preferred_element_type=jnp.float32)
                + b_re.astype(jnp.float32)).reshape(T, N_GROUPS, EXPERTS_PER_GROUP)
    e_logits = jnp.take_along_axis(e_logits, g_sel[:, None, None], axis=1)[:, 0]
    e_prob = jax.nn.softmax(e_logits, axis=-1)
    top_p, top_i = lax.top_k(e_prob, TOP_K_IN_GROUP)
    wts = top_p / jnp.sum(top_p, axis=-1, keepdims=True) * g_w
    eidx = g_sel[:, None] * EXPERTS_PER_GROUP + top_i

    A = T * TOP_K_IN_GROUP
    e_flat = eidx.reshape(A).astype(jnp.int32)
    tok_flat = jnp.repeat(jnp.arange(T, dtype=jnp.int32), TOP_K_IN_GROUP)
    w_flat = wts.reshape(A).astype(h.dtype)
    order = jnp.argsort(e_flat, stable=True)
    e_s, tok_s, w_s = e_flat[order], tok_flat[order], w_flat[order]
    counts = jnp.zeros((N_EXPERTS,), jnp.int32).at[e_flat].add(1)
    padded = (counts + ROW_BLOCK - 1) // ROW_BLOCK * ROW_BLOCK
    start = jnp.cumsum(counts) - counts
    pad_end = jnp.cumsum(padded)
    pstart = pad_end - padded
    dest = pstart[e_s] + jnp.arange(A, dtype=jnp.int32) - start[e_s]
    n_rows = A + N_EXPERTS * ROW_BLOCK
    n_blk = n_rows // ROW_BLOCK
    row_tok = jnp.zeros((n_rows,), jnp.int32).at[dest].set(tok_s)
    row_w = jnp.zeros((n_rows,), h.dtype).at[dest].set(w_s)
    blk_exp = jnp.clip(jnp.searchsorted(pad_end, jnp.arange(n_blk, dtype=jnp.int32) * ROW_BLOCK,
                                        side="right"), 0, N_EXPERTS - 1)

    def expert_block(args):
        toks, wb, e = args
        xb = hf[toks]
        hid = jax.nn.silu(jnp.matmul(xb, w_g[e])) * jnp.matmul(xb, w_u[e])
        return jnp.matmul(hid, w_d[e]) * wb[:, None]

    yb = lax.map(expert_block, (row_tok.reshape(n_blk, ROW_BLOCK),
                                row_w.reshape(n_blk, ROW_BLOCK), blk_exp))
    y = jnp.zeros_like(hf).at[row_tok].add(yb.reshape(n_rows, D))
    return y.reshape(B, S, D)

def first_inputs(seed: int = 0) -> dict:
    key = jax.random.key(seed)
    ks = jax.random.split(key, 26)
    f32 = jnp.float32

    def nrm(k, shape, scale):
        return jax.random.normal(k, shape, f32) * scale

    L, D, C = DEPTH, D_MODEL, CONV_CH
    return {
        "x": nrm(ks[0], (BATCH, SEQ, D), 1.0),
        "attn_norm_g": 1.0 + nrm(ks[1], (L, D), 0.05),
        "w_in": nrm(ks[2], (L, D, IN_COLS), D ** -0.5),
        "conv_dw_w": nrm(ks[3], (L, CONV_WIDTH, C), CONV_WIDTH ** -0.5),
        "conv_dw_b": nrm(ks[4], (L, C), 0.02),
        "conv_ln_g": 1.0 + nrm(ks[5], (L, C), 0.05),
        "conv_ln_b": nrm(ks[6], (L, C), 0.02),
        "w_conv_out": nrm(ks[7], (L, C, D), C ** -0.5),
        "q_norm_g": 1.0 + nrm(ks[8], (L, DA_HEAD_DIM), 0.05),
        "k_norm_g": 1.0 + nrm(ks[9], (L, DA_HEAD_DIM), 0.05),
        "lambda_q1": nrm(ks[10], (L, DA_HEAD_DIM), 0.1),
        "lambda_k1": nrm(ks[11], (L, DA_HEAD_DIM), 0.1),
        "lambda_q2": nrm(ks[12], (L, DA_HEAD_DIM), 0.1),
        "lambda_k2": nrm(ks[13], (L, DA_HEAD_DIM), 0.1),
        "subln_g": 1.0 + nrm(ks[14], (L, DA_V_DIM), 0.05),
        "w_attn_out": nrm(ks[15], (L, ATTN_W, D), ATTN_W ** -0.5),
        "w_out": nrm(ks[16], (L, D, D), D ** -0.5),
        "ffn_norm_g": 1.0 + nrm(ks[17], (L, D), 0.05),
        "w_router_group": nrm(ks[18], (L, D, N_GROUPS), D ** -0.5),
        "b_router_group": nrm(ks[19], (L, N_GROUPS), 0.01),
        "w_router_expert": nrm(ks[20], (L, D, N_EXPERTS), D ** -0.5),
        "b_router_expert": nrm(ks[21], (L, N_EXPERTS), 0.01),
        "w_gate_e": nrm(ks[22], (L, N_EXPERTS, D, D_EXPERT), D ** -0.5),
        "w_up_e": nrm(ks[23], (L, N_EXPERTS, D, D_EXPERT), D ** -0.5),
        "w_down_e": nrm(ks[24], (L, N_EXPERTS, D_EXPERT, D), D_EXPERT ** -0.5),
    }

def first_block(x, attn_norm_g, w_in, conv_dw_w, conv_dw_b, conv_ln_g, conv_ln_b, w_conv_out,
              q_norm_g, k_norm_g, lambda_q1, lambda_k1, lambda_q2, lambda_k2, subln_g,
              w_attn_out, w_out, ffn_norm_g, w_router_group, b_router_group,
              w_router_expert, b_router_expert, w_gate_e, w_up_e, w_down_e):
    B, S, D = x.shape
    for l in range(DEPTH):
        lam_init = 0.8 - 0.6 * math.exp(-0.3 * l)
        h = rms_norm(x, attn_norm_g[l])
        proj = jnp.matmul(h, w_in[l])
        o0 = COL_CONV
        o1 = o0 + COL_Q
        o2 = o1 + COL_K
        o3 = o2 + COL_V
        u_conv = proj[..., :o0]
        q = proj[..., o0:o1].reshape(B, S, DA_HEADS, 2, DA_HEAD_DIM)
        k = proj[..., o1:o2].reshape(B, S, DA_HEADS, 2, DA_HEAD_DIM)
        v = proj[..., o2:o3].reshape(B, S, DA_HEADS, DA_V_DIM)
        gates = jax.nn.sigmoid(proj[..., o3:]).reshape(B, S, N_BRANCH, D)

        conv_out = conformer_conv(u_conv, conv_dw_w[l], conv_dw_b[l], conv_ln_g[l], conv_ln_b[l])

        q = rms_norm(q, q_norm_g[l])
        k = rms_norm(k, k_norm_g[l])
        lam = (jnp.exp(jnp.sum(lambda_q1[l].astype(jnp.float32) * lambda_k1[l].astype(jnp.float32)))
               - jnp.exp(jnp.sum(lambda_q2[l].astype(jnp.float32) * lambda_k2[l].astype(jnp.float32)))
               + lam_init)
        attn_out = diff_attention(q, k, v, lam, subln_g[l], lam_init)

        merged = (gates[:, :, 0] * jnp.matmul(conv_out, w_conv_out[l])
                  + gates[:, :, 1] * jnp.matmul(attn_out, w_attn_out[l]))
        x = x + jnp.matmul(merged, w_out[l])
        h2 = rms_norm(x, ffn_norm_g[l])
        x = x + hierarchical_moe(h2, w_router_group[l], b_router_group[l], w_router_expert[l],
                                 b_router_expert[l], w_gate_e[l], w_up_e[l], w_down_e[l])
    return x


HEAD_DIM = 64
GROUP_WIDTH = D_MODEL // 4
MIX_WIDTH = 4 * GROUP_WIDTH
N_GROUP_HEADS = GROUP_WIDTH // HEAD_DIM
SHORT_CONV_K = 3
DSWA_CONFIGS = ((128, 1), (512, 4), (2048, 16))
POOL_WINDOWS = (2, 4, 8, 16)
POOL_GROUP = GROUP_WIDTH // len(POOL_WINDOWS)
ROPE_THETA = 500000.0
ROPE_DIM = HEAD_DIM // 4
MEM_LEN = 256
XA_HEADS = 4
XA_HEAD_DIM = D_MODEL // XA_HEADS
D_FF = ((8 * D_MODEL // 3 + 127) // 128) * 128
FFN_CONV_K = 3
RMS_EPS = 1e-6
NEG_INF = -1e30
FORGET_BIAS_INIT = 3.0
N_IN = 3 * GROUP_WIDTH + 3 * GROUP_WIDTH + 3 * GROUP_WIDTH + N_GROUP_HEADS + GROUP_WIDTH


def rms_norm_2(t, g):
    tf = t.astype(jnp.float32)
    y = tf * lax.rsqrt(jnp.mean(tf * tf, axis=-1, keepdims=True) + RMS_EPS)
    return (y * g.astype(jnp.float32)).astype(t.dtype)

def causal_depthwise_conv(t, w):
    K, C = w.shape
    return lax.conv_general_dilated(
        t, w.astype(t.dtype)[:, None, :], window_strides=(1,), padding=((K - 1, 0),),
        dimension_numbers=("NWC", "WIO", "NWC"), feature_group_count=C)

def to_heads(t):
    B, S, W = t.shape
    return t.reshape(B, S, W // HEAD_DIM, HEAD_DIM).transpose(0, 2, 1, 3)

def from_heads(t):
    B, H, S, dh = t.shape
    return t.transpose(0, 2, 1, 3).reshape(B, S, H * dh)

def rope_tables(positions):
    inv_freq = ROPE_THETA ** (-jnp.arange(0, ROPE_DIM, 2, dtype=jnp.float32) / ROPE_DIM)
    ang = positions.astype(jnp.float32)[:, None, :, None] * inv_freq
    return jnp.cos(ang), jnp.sin(ang)

def apply_partial_rope(t, cos, sin):
    tf = t.astype(jnp.float32)
    r1, r2 = jnp.split(tf[..., :ROPE_DIM], 2, axis=-1)
    rot = jnp.concatenate([r1 * cos - r2 * sin, r2 * cos + r1 * sin], axis=-1)
    return jnp.concatenate([rot, tf[..., ROPE_DIM:]], axis=-1).astype(t.dtype)

def short_conv_mixer(p, w_conv):
    h, b_gate, c_gate = jnp.split(p, 3, axis=-1)
    return b_gate * causal_depthwise_conv(c_gate * h, w_conv)

def dilated_attention(q, k, v):
    B, H, S, dh = q.shape
    nb = S // Q_BLOCK
    qb = q.reshape(B, H, nb, Q_BLOCK, dh).transpose(2, 0, 1, 3, 4)
    kf = k.astype(jnp.float32)
    vf = v.astype(jnp.float32)
    scale = dh ** -0.5

    def block(args):
        i, qi = args
        t = i * Q_BLOCK + jnp.arange(Q_BLOCK)
        qs = qi.astype(jnp.float32) * scale
        scores, values = [], []
        for window, dil in DSWA_CONFIGS:
            idx = t[:, None] - dil * jnp.arange(window // dil + 1)[None, :]
            idxc = jnp.maximum(idx, 0)
            kg = kf[:, :, idxc]
            s = jnp.einsum("bhqd,bhqnd->bhqn", qs, kg)
            scores.append(jnp.where(idx >= 0, s, NEG_INF))
            values.append(vf[:, :, idxc])
        m = functools.reduce(jnp.maximum, [s.max(axis=-1, keepdims=True) for s in scores])
        num, den = 0.0, 0.0
        for s, vg in zip(scores, values):
            e = jnp.exp(s - m)
            num = num + jnp.einsum("bhqn,bhqnd->bhqd", e, vg)
            den = den + e.sum(axis=-1, keepdims=True)
        return num / den

    o = lax.map(block, (jnp.arange(nb), qb))
    return o.transpose(1, 2, 0, 3, 4).reshape(B, H, S, dh).astype(q.dtype)

def dilated_mixer(p, cos, sin):
    q, k, v = [to_heads(t) for t in jnp.split(p, 3, axis=-1)]
    q = apply_partial_rope(q, cos, sin)
    k = apply_partial_rope(k, cos, sin)
    return from_heads(dilated_attention(q, k, v))

def forgetting_attention(q, k, v, c):
    B, H, S, dh = q.shape
    nb = S // Q_BLOCK
    qb = q.reshape(B, H, nb, Q_BLOCK, dh).transpose(2, 0, 1, 3, 4)
    cb = c.reshape(B, H, nb, Q_BLOCK).transpose(2, 0, 1, 3)
    kf = k.astype(jnp.float32)
    vf = v.astype(jnp.float32)
    kpos = jnp.arange(S)
    scale = dh ** -0.5

    def block(args):
        i, qi, ci = args
        t = i * Q_BLOCK + jnp.arange(Q_BLOCK)
        s = jnp.einsum("bhqd,bhkd->bhqk", qi.astype(jnp.float32) * scale, kf)
        s = s + ci[..., None] - c[:, :, None, :]
        s = jnp.where(kpos[None, :] <= t[:, None], s, NEG_INF)
        return jnp.einsum("bhqk,bhkd->bhqd", jax.nn.softmax(s, axis=-1), vf)

    o = lax.map(block, (jnp.arange(nb), qb, cb))
    return o.transpose(1, 2, 0, 3, 4).reshape(B, H, S, dh).astype(q.dtype)

def forgetting_mixer(p, b_f):
    G = GROUP_WIDTH
    q, k, v = to_heads(p[..., :G]), to_heads(p[..., G:2 * G]), to_heads(p[..., 2 * G:3 * G])
    logf = jax.nn.log_sigmoid(p[..., 3 * G:].astype(jnp.float32) + b_f.astype(jnp.float32))
    c = jnp.cumsum(logf, axis=1).transpose(0, 2, 1)
    return from_heads(forgetting_attention(q, k, v, c))

def pool_mixer(p, w_pool, scale):
    B, S, _ = p.shape
    pf = p.astype(jnp.float32).reshape(B, S, len(POOL_WINDOWS), POOL_GROUP)
    cs = jnp.cumsum(pf, axis=1)
    cs0 = jnp.concatenate([jnp.zeros_like(cs[:, :1]), cs], axis=1)
    t = jnp.arange(S)
    outs = []
    for g, w in enumerate(POOL_WINDOWS):
        upper = cs0[:, 1:, g]
        lower = cs0[:, jnp.maximum(t + 1 - w, 0), g]
        cnt = jnp.minimum(t + 1, w).astype(jnp.float32)[None, :, None]
        outs.append((upper - lower) / cnt - pf[:, :, g])
    z = jnp.stack(outs, axis=2)
    y = jnp.einsum("bsgc,gcd->bsgd", z, w_pool.astype(jnp.float32)).reshape(B, S, GROUP_WIDTH)
    return (y * scale.astype(jnp.float32)).astype(p.dtype)

def memory_cross_attention(xn, memn, w_q, w_kv, w_o):
    B, S, D = xn.shape
    M = memn.shape[1]
    q = (xn @ w_q).reshape(B, S, XA_HEADS, XA_HEAD_DIM)
    k, v = jnp.split(memn @ w_kv, 2, axis=-1)
    k = k.reshape(B, M, XA_HEADS, XA_HEAD_DIM)
    v = v.reshape(B, M, XA_HEADS, XA_HEAD_DIM)
    s = jnp.einsum("bshd,bmhd->bhsm", q.astype(jnp.float32), k.astype(jnp.float32)) * XA_HEAD_DIM ** -0.5
    o = jnp.einsum("bhsm,bmhd->bshd", jax.nn.softmax(s, axis=-1), v.astype(jnp.float32))
    return o.reshape(B, S, D).astype(xn.dtype) @ w_o

def conv_ffn(xn, w_up, w_conv, w_down):
    u = causal_depthwise_conv(xn @ w_up, w_conv)
    a, g = jnp.split(u, 2, axis=-1)
    return (a * jax.nn.silu(g)) @ w_down

def second_inputs(seed: int = 0) -> dict:
    key = jax.random.key(seed)
    ks = jax.random.split(key, 24)
    f32 = jnp.float32
    nrm = lambda k, shape, s: jax.random.normal(k, shape, f32) * s
    L, D, G = DEPTH, D_MODEL, GROUP_WIDTH
    x = jax.random.normal(ks[0], (BATCH, SEQ, D), f32)
    mem = jax.random.normal(ks[1], (BATCH, MEM_LEN, D), f32)
    offset = jax.random.randint(ks[2], (BATCH, 1), 0, 1024, dtype=jnp.int32)
    positions = (jnp.arange(SEQ, dtype=jnp.int32)[None, :] + offset).astype(jnp.int32)
    return {
        "x": x,
        "mem": mem,
        "positions": positions,
        "g_mix": 1.0 + nrm(ks[3], (L, D), 0.02),
        "w_in": nrm(ks[4], (L, D, N_IN), D ** -0.5),
        "b_forget": FORGET_BIAS_INIT + nrm(ks[5], (L, N_GROUP_HEADS), 0.1),
        "w_sconv": nrm(ks[6], (L, SHORT_CONV_K, G), SHORT_CONV_K ** -0.5),
        "w_pool": nrm(ks[7], (L, len(POOL_WINDOWS), POOL_GROUP, POOL_GROUP), POOL_GROUP ** -0.5),
        "pool_scale": 1.0 + nrm(ks[8], (L, G), 0.02),
        "w_out": nrm(ks[9], (L, MIX_WIDTH, D), MIX_WIDTH ** -0.5),
        "g_xa": 1.0 + nrm(ks[10], (L, D), 0.02),
        "g_mem": 1.0 + nrm(ks[11], (L, D), 0.02),
        "w_xq": nrm(ks[12], (L, D, D), D ** -0.5),
        "w_xkv": nrm(ks[13], (L, D, 2 * D), D ** -0.5),
        "w_xo": nrm(ks[14], (L, D, D), D ** -0.5),
        "g_ffn": 1.0 + nrm(ks[15], (L, D), 0.02),
        "w_up": nrm(ks[16], (L, D, 2 * D_FF), D ** -0.5),
        "w_ffconv": nrm(ks[17], (L, FFN_CONV_K, 2 * D_FF), FFN_CONV_K ** -0.5),
        "w_down": nrm(ks[18], (L, D_FF, D), D_FF ** -0.5),
        "g_final": 1.0 + nrm(ks[19], (D,), 0.02),
    }

def second_block(x, mem, positions, g_mix, w_in, b_forget, w_sconv, w_pool, pool_scale, w_out,
              g_xa, g_mem, w_xq, w_xkv, w_xo, g_ffn, w_up, w_ffconv, w_down, g_final):
    G = GROUP_WIDTH
    cos, sin = rope_tables(positions)
    h = x
    for l in range(DEPTH):
        xn = rms_norm_2(h, g_mix[l])
        proj = xn @ w_in[l]
        pa, pb, pc, pd = jnp.split(proj, [3 * G, 6 * G, 9 * G + N_GROUP_HEADS], axis=-1)
        ya = short_conv_mixer(pa, w_sconv[l])
        yb = dilated_mixer(pb, cos, sin)
        yc = forgetting_mixer(pc, b_forget[l])
        yd = pool_mixer(pd, w_pool[l], pool_scale[l])
        h = h + jnp.concatenate([ya, yb, yc, yd], axis=-1) @ w_out[l]
        h = h + memory_cross_attention(rms_norm_2(h, g_xa[l]), rms_norm_2(mem, g_mem[l]),
                                       w_xq[l], w_xkv[l], w_xo[l])
        h = h + conv_ffn(rms_norm_2(h, g_ffn[l]), w_up[l], w_ffconv[l], w_down[l])
    return rms_norm_2(h, g_final)


def setup_inputs(seed=0):
    out = dict(first_inputs(seed))
    for name, value in second_inputs(seed + 1).items():
        if name != "x":
            out[name + "_2"] = value
    return out


def reference(
    x, attn_norm_g, w_in, conv_dw_w, conv_dw_b, conv_ln_g, conv_ln_b, w_conv_out, q_norm_g,
    k_norm_g, lambda_q1, lambda_k1, lambda_q2, lambda_k2, subln_g, w_attn_out, w_out,
    ffn_norm_g, w_router_group, b_router_group, w_router_expert, b_router_expert, w_gate_e,
    w_up_e, w_down_e, mem_2, positions_2, g_mix_2, w_in_2, b_forget_2, w_sconv_2, w_pool_2,
    pool_scale_2, w_out_2, g_xa_2, g_mem_2, w_xq_2, w_xkv_2, w_xo_2, g_ffn_2, w_up_2,
    w_ffconv_2, w_down_2, g_final_2,
):
    x = first_block(
        x, attn_norm_g, w_in, conv_dw_w, conv_dw_b, conv_ln_g, conv_ln_b, w_conv_out, q_norm_g,
        k_norm_g, lambda_q1, lambda_k1, lambda_q2, lambda_k2, subln_g, w_attn_out, w_out,
        ffn_norm_g, w_router_group, b_router_group, w_router_expert, b_router_expert, w_gate_e,
        w_up_e, w_down_e,
    )
    return second_block(
        x, mem_2, positions_2, g_mix_2, w_in_2, b_forget_2, w_sconv_2, w_pool_2, pool_scale_2,
        w_out_2, g_xa_2, g_mem_2, w_xq_2, w_xkv_2, w_xo_2, g_ffn_2, w_up_2, w_ffconv_2,
        w_down_2, g_final_2,
    )


_drawn_inputs = setup_inputs


def setup_inputs(seed=0):
    import zlib

    import numpy as np

    out = dict(_drawn_inputs(seed))
    spreads = {}
    factors = {'conv_ln_b': 2.8,
     'lambda_q1': 3.451,
     'b_router_group': 3.178,
     'b_router_expert': 3.179,
     'g_mix_2': 3.519,
     'b_forget_2': 64.0,
     'pool_scale_2': 8.0,
     'g_xa_2': 8.0,
     'g_mem_2': 8.0,
     'g_ffn_2': 18.015}
    for name, (base, spread) in spreads.items():
        noise = np.random.default_rng([zlib.crc32(name.encode()), seed]).standard_normal(out[name].shape)
        drawn = base * np.exp(spread * noise) if base else spread * noise
        out[name] = __import__('jax').numpy.asarray(drawn.astype(out[name].dtype))
    for name, factor in factors.items():
        out[name] = (out[name] * factor).astype(out[name].dtype)
    return out
```

```python
from contextlib import ExitStack

import numpy as np
import concourse.bass as bass
from concourse import mybir

F32 = mybir.dt.float32
I32 = mybir.dt.int32
ALU = mybir.AluOpType
ACT = mybir.ActivationFunctionType
AX = mybir.AxisListType.X

P = 128
T = 256
D = 1024
DC = D // P
TT = T // P
CW = 31
NE, NG, EG = 32, 4, 8
CAP = 32
QUAD = P // CAP
QUADS = NE // QUAD
ROUNDS = T // CAP
FF = 2816
FC = FF // P
RING = 6
UW = DC * 512
EUNITS = 12
EPS = 1e-6
BIG = 1e30
PRE_UNITS = 13
POOLS = (2, 4, 8, 16)
LAM0 = 0.2
MAGIC = 12582912.0
TWO_PI = (6.28125, 0.0019340515136718750, 2 * np.pi - 6.28125 - 0.0019340515136718750)


def constants():
    cols, at, n = [], {}, 0

    def add(name, a):
        nonlocal n
        a = np.asarray(a, np.float32).reshape(P, -1)
        at[name] = (n, n + a.shape[1])
        cols.append(a)
        n += a.shape[1]

    p = np.arange(P)
    add("ident", np.eye(P))
    add("ones", np.ones((P, P)))
    add("blk64", p[:, None] // 64 == p[None, :] // 64)
    add("before", p[:, None] < p[None, :])
    rot = np.zeros((P, P))
    for m in range(P):
        if m % 64 < 8:
            rot[m + 8, m] = -1.0
        elif m % 64 < 16:
            rot[m - 8, m] = 1.0
    add("rot", rot)
    d = (np.arange(TT)[None, :, None] * P + p[:, None, None]) - np.arange(T)[None, None, :]
    add("causal", np.where(d >= 0, 0.0, -BIG))
    mult = sum(((d >= 0) & (d % dil == 0) & (d <= w)).astype(np.float32) for w, dil in ((128, 1), (512, 4), (2048, 16)))
    add("dil_mask", np.where(mult > 0, 0.0, -BIG))
    add("dil_mult", mult)
    w = np.array([[POOLS[2 * c + (q >= 64)] for c in range(2)] for q in p])
    add("inv_count", 1.0 / np.minimum(np.arange(T)[None, None, :] + 1, w[:, :, None]))
    sel = np.zeros((P, 4, P))
    for h in range(4):
        sel[h, h, :] = 1.0
    add("sel", sel)
    f = np.float32(500000.0) ** (-np.arange(0, 16, 2, dtype=np.float32) / np.float32(16))
    add("inv_freq", [f[q % 8] if q % 64 < 16 else 0.0 for q in p])
    add("iota", np.tile(np.arange(CAP), (P, 1)))
    add("round_start", np.tile(np.arange(ROUNDS) * CAP, (P, 1)))
    add("falling", np.tile(8.0 - np.arange(8), (P, 1)))
    add("halves", np.stack([p < 64, p >= 64], 1))
    add("eighth", np.stack([p < 64, p >= 64], 1) / 8.0)
    add("neg_half", np.full((P, 1), -0.5))
    return np.concatenate(cols, 1), at


PARAMS = [("g1", 8), ("taps", 4 * CW), ("conv_b", 4), ("ln_g", 4), ("ln_b", 4), ("q_g", 1), ("k_g", 1), ("sub_g", 1),
          ("g2", 8), ("w_r", DC * 36), ("b_r", 36), ("lam_q", 1), ("lam_k", 1), ("g_mix", 8), ("b_f", 1), ("w_sc", 6),
          ("w_pool", 256), ("pool_g", 2), ("g_xa", 8), ("g_mem", 8), ("g_ffn", 8), ("ff_taps", 2 * FC * 3), ("g_fin", 8)]


def param_places():
    at, n = {}, 0
    for name, w in PARAMS:
        at[name] = (n, n + w)
        n += w
    return at, n


def psum_plan():
    uses = [("xT", i) for i in range(4)] + [("lam", 0), ("n1", 0)]
    uses += [(k, m) for k in ("ca", "cg", "q", "k") for m in range(4)]
    uses += [("v", t) for t in range(2)] + [(k, i) for k in ("qn", "kn") for i in range(2)]
    uses += [("s1", i) for i in range(8)] + [("gt", m) for m in range(16)]
    uses += [("aT1", h) for h in range(4)] + [("o1", h) for h in range(4)] + [("on", i) for i in range(2)]
    uses += [("mu", 0), ("var", 0)]
    uses += [(k, m) for k in ("co", "ao", "wo") for m in range(8)]
    uses += [("n2", 0), ("rt", 0), ("rt", 1)] + [("h2t", i) for i in range(4)] + [("pos", 0), ("pos", 1), ("cnt", 0)]
    uses += [("posb", 0), ("nmix", 0)]
    uses += [("pa", m) for m in range(6)] + [("qb", m) for m in range(2)] + [("kb", m) for m in range(2)]
    uses += [("vb", t) for t in range(2)] + [(k, m) for k in ("qc", "kc") for m in range(2)]
    uses += [("vc", t) for t in range(2)] + [("pd", m) for m in range(2)] + [("f", 0)]
    uses += [("rq", 0), ("rk", 0)] + [("sb", i) for i in range(4)] + [("sc", i) for i in range(4)] + [("pl", 0)]
    uses += [("aTb", h) for h in range(4)] + [("ob", h) for h in range(2)]
    uses += [("aTc", h) for h in range(4)] + [("oc", h) for h in range(2)]
    uses += [("w2", m) for m in range(8)]
    uses += [("mT", i) for i in range(4)] + [("nxa", 0), ("nmem", 0)] + [("kx", m) for m in range(8)] + [("vx", i) for i in range(4)]
    uses += [("qx", m) for m in range(8)] + [("sx", i) for i in range(4)]
    uses += [("aTx", h) for h in range(4)] + [("ox", h) for h in range(4)] + [("xo", m) for m in range(8)]
    uses += [("nffn", 0)] + [(k, i) for i in range(11) for k in ("ua", "ug")] + [("dn", m) for m in range(8)]
    uses += [("nfin", 0)] + [("out", i) for i in range(4)]
    place, turn = {}, [0] * 8
    for i, u in enumerate(uses):
        turn[i % 8] += 1
        place[u] = (i % 8, turn[i % 8])
    return place


def two_blocks_kernel(nc, A, out, CAT):
    PAT, PW = param_places()
    PLACE = psum_plan()
    CWID = max(b for _, b in CAT.values())

    with ExitStack() as ctx:
        def sb(name, words, dt=F32):
            return ctx.enter_context(nc.sbuf_tensor(name, [P, words], dt))

        def sem(name):
            return ctx.enter_context(nc.semaphore(name))

        ring = [sb(f"ring{i}", UW) for i in range(RING)]
        const = sb("const", CWID)
        par = sb("par", PW)
        xT = sb("xT", DC * T)
        hT = sb("hT", DC * T)
        sq = sb("sq", DC * T)
        big = sb("big", FC * T)
        qko = sb("qko", 12 * T)
        vtok = sb("vtok", TT * 512)
        mrg = sb("mrg", DC * T)
        pad = sb("pad", 4 * (T + CW - 1))
        att = sb("att", 16 * T)
        rs2 = [sb(f"rs{i}", 512) for i in range(2)]
        st = sb("st", 128)
        w_f = sb("w_f", DC * 4)
        count_i = sb("count_i", 1, I32)
        bank = [ctx.enter_context(nc.psum_tensor(f"bank{i}", [P, 512], F32)) for i in range(8)]

        def C(name, parts=slice(0, P)):
            a, b = CAT[name]
            return const[parts, a:b]

        def W(name, parts=slice(0, P)):
            a, b = PAT[name]
            return par[parts, a:b]

        def col(name, i, parts=slice(0, P)):
            a, _ = PAT[name]
            return par[parts, a + i:a + i + 1]

        def ch(t, i, n=1, w=T):
            v = t[:, i * w:(i + n) * w]
            return v if n == 1 else v.rearrange("p (c t) -> p c t", c=n)

        def flat(t, a, n):
            return t[:, a:a + n]

        full = [sem(f"bank_full{i}") for i in range(8)]
        empty = [sem(f"bank_empty{i}") for i in range(8)]
        landed = [sem(f"weights_landed{i}") for i in range(RING)]
        used = [sem(f"weights_used{i}") for i in range(RING)]
        landed_post = [sem(f"weights_landed_post{i}") for i in range(RING)]
        used_post = [sem(f"weights_used_post{i}") for i in range(RING)]
        names = """const_in par_in x_in pos_in wf_in mem_in out_done dve_step act_step zeroed squares normed lam_in
                   lam_exp qk_ready s_max s_exp a_ready conved conv_dev conv_z conv_sig conv_out attn_out merged
                   logits pair_gap g_exp e_exp member rounds picked pick_step hid_step swt_full rows_full swt rows gate_sig
                   hidden hid_full hidT y_out comb_full added experts_done pos_f ang trig rope rows_zero f_abs f_exp
                   c_rows z_pool y_mix pads_zero up_conv up_sig up_act""".split()
        S = {n: sem(n) for n in names}
        count = {}

        def signal(ins, name, by=1):
            ins.then_inc(S[name], by)
            count[name] = count.get(name, 0) + by
            return count[name]

        def done(eng, ins, name):
            eng.wait_ge(S[name], signal(ins, name))

        def begin(pe, use):
            b, n = PLACE[use]
            if n > 1:
                pe.wait_ge(empty[b], n - 1)
            return bank[b]

        def filled(ins, use):
            ins.then_inc(full[PLACE[use][0]], 1)

        def arrive(eng, use):
            b, n = PLACE[use]
            eng.wait_ge(full[b], n)
            return bank[b]

        def emptied(ins, use):
            ins.then_inc(empty[PLACE[use][0]], 1)

        def copied(eng, use):
            b, n = PLACE[use]
            eng.wait_ge(empty[b], n)

        w_in = A["w_in"][0].rearrange("(k p) n -> p k n", p=P)
        w_co = A["w_conv_out"][0].rearrange("(k p) n -> p k n", p=P)
        w_ao = A["w_attn_out"][0].rearrange("(k p) n -> p k n", p=P)
        w_o = A["w_out"][0].rearrange("(k p) n -> p k n", p=P)
        pre = [w_in[:, :, 512 * i:512 * i + 512] for i in range(9)] + [w_co, w_ao]
        pre += [w_o[:, :, 512 * i:512 * i + 512] for i in range(2)]
        assert len(pre) == PRE_UNITS
        w_in2 = A["w_in_2"][0].rearrange("(k p) n -> p k n", p=P)
        w_o2 = A["w_out_2"][0].rearrange("(k p) n -> p k n", p=P)
        w_xkv = A["w_xkv_2"][0].rearrange("(k p) n -> p k n", p=P)
        w_xq = A["w_xq_2"][0].rearrange("(k p) n -> p k n", p=P)
        w_xo = A["w_xo_2"][0].rearrange("(k p) n -> p k n", p=P)
        w_up = A["w_up_2"][0].rearrange("(k p) (a n) -> p k a n", p=P, a=2)
        w_dn = A["w_down_2"][0].rearrange("(k p) n -> p k n", p=P)

        def halves(w, i):
            return [w[:, :, 512 * i:512 * i + 512]]

        post = [halves(w_in2, i) for i in range(4)] + [[w_in2[:, :, 2048:2304], w_in2[:, :, 2308:2564]]]
        post += [halves(w_o2, i) for i in range(2)] + [halves(w_xkv, i) for i in range(4)]
        post += [halves(w_xq, i) for i in range(2)] + [halves(w_xo, i) for i in range(2)]
        FIRST_UP = len(post)
        post += [[w_up[:, :, a, 256 * i:256 * i + 256] for a in range(2)] for i in range(11)]
        FIRST_DN = len(post)
        post += [[w_dn[:, 4 * i:min(4 * i + 4, FC), :]] for i in range(6)]
        parts_landed = {}
        seen = [0] * RING
        for j, u in enumerate(post):
            s = (PRE_UNITS + j) % RING
            seen[s] += 16 * len(u)
            parts_landed[j] = seen[s]

        def pre_unit(pe, i):
            pe.wait_ge(landed[i % RING], 16 * (i // RING + 1))
            return ring[i % RING]

        def post_unit(pe, j):
            s = (PRE_UNITS + j) % RING
            pe.wait_ge(landed_post[s], parts_landed[j])
            return ring[s]

        def u512(slot):
            return slot[:, :].rearrange("p (k n) -> p k n", k=8)

        def u1024(slot):
            return slot[:, :].rearrange("p (k n) -> p k n", k=4)

        o = 0

        def carve(n):
            nonlocal o
            o += n
            return big[:, o - n:o]

        xeT = carve(DC * P).rearrange("p (k s) -> p k s", k=DC)
        sig = carve(512)
        hid = carve(512)
        hidT = carve(512).rearrange("p (k s) -> p k s", k=4)
        y_e = carve(D)
        swT = carve(T)
        pick = carve(TT * P).rearrange("p (t j s) -> p t j s", t=TT, j=QUAD)
        wpick = carve(TT * P).rearrange("p (t j s) -> p t j s", t=TT, j=QUAD)
        slot_of = carve(TT * ROUNDS * NE).rearrange("p (t r) -> p t r", t=TT)
        weight_of = carve(TT * ROUNDS * NE).rearrange("p (t r) -> p t r", t=TT)
        h2tok = ch(att, 0, TT, D)
        NORMS = {n: 8 * i for i, n in enumerate(("n1", "n2", "nmix", "nxa", "nmem", "nffn", "nfin"))}
        SQUARES = {n: 2 * i for i, n in enumerate(("n1", "qn", "kn", "on", "var", "n2", "nmix", "nxa", "nmem", "nffn", "nfin"))}
        ROOTS = [(("n1", 0), T, D)] + [((k, i), 512, n) for k, n in (("qn", 64), ("kn", 64), ("on", P)) for i in range(2)]
        ROOTS += [(("var", 0), T, 512)] + [((k, 0), T, D) for k in ("n2", "nmix", "nxa", "nmem", "nffn", "nfin")]
        TURN = {use: i % 2 for i, (use, _, _) in enumerate(ROOTS)}


        ro = 0

        def small(*shape):
            nonlocal ro
            n = int(np.prod(shape))
            v = qko[:, ro:ro + n]
            ro += n
            if len(shape) == 1:
                return v
            names = "abc"[:len(shape)]
            return v.rearrange(f"p ({' '.join(names)}) -> p {' '.join(names)}", **dict(zip(names, shape)))

        member = small(TT, NG, EG)
        e_all = small(TT, NG, EG)
        logit = small(TT, 36)
        place_of = small(TT, NE)
        g_hot, g_tmp = small(TT, NG), small(TT, NG)
        g_gap = small(TT * NG)
        g_gap3 = g_gap.rearrange("p (t g) -> p t g", t=TT)
        e_val, e_tmp, hot1, hot2 = (small(TT, EG) for _ in range(4))
        g_max, g_sum, e_max1, e_max2, e_gap, w_1, w_2, tie = (small(TT) for _ in range(8))
        assert ro <= 2048
        pool_x = qko[:, 0:544].rearrange("p (c t) -> p c t", c=2)
        pool_s = [qko[:, 544 * i:544 * i + 544].rearrange("p (c t) -> p c t", c=2) for i in (1, 2)]
        z_pool = qko[:, 1632:2144]
        conv_x = pad[:, 512:1028].rearrange("p (c t) -> p c t", c=2)
        f_z, f_abs, f_e = (big[0:4, 4612 + T * i:4612 + T * i + T] for i in range(3))
        c_rows = qko[:, 2144:2144 + 2 * T]
        c_row, neg_c = (c_rows[:, T * i:T * i + T] for i in range(2))
        f_zero = qko[0:4, 2144 + 2 * T:2144 + 3 * T]
        qc_head = [ch(big, i) for i in (10, 11, 16, 17)]
        st_pos = rs2[0][:, 0:T]
        pos_i = att[0:1, 3072:3072 + T].bitcast(I32)
        up_x = pad[:, 0:4 * (T + 2)].rearrange("p (c t) -> p c t", c=4)
        up_y, up_s = att[:, 0:1024], att[:, 1024:1536]

        block = ctx.enter_context(nc.Block())

        @block.sync
        def _(sp):
            sp.dma_start(const[:, :], A["const"]).then_inc(S["const_in"], 16)
            sp.dma_start(par[:, :], A["par"]).then_inc(S["par_in"], 16)
            for i, src in enumerate(pre):
                if i >= RING:
                    sp.wait_ge(used[i % RING], i // RING)
                dst = ring[i % RING][:, :].rearrange("p (k n) -> p k n", k=src.shape[1])
                sp.dma_start(dst, src).then_inc(landed[i % RING], 16)

            w_g = A["w_gate_e"][0].rearrange("(q j) (u p c) n -> q u p j (c n)", j=QUAD, c=2, p=P)
            w_u = A["w_up_e"][0].rearrange("(q j) (u p c) n -> q u p j (c n)", j=QUAD, c=2, p=P)
            w_d = A["w_down_e"][0].rearrange("(q j) (u p) n -> q u p j n", j=QUAD, p=P)

            def step(q, n):
                for u in range(EUNITS):
                    i = PRE_UNITS + u
                    s = i % RING
                    sp.wait_ge(used[s], n * (EUNITS // RING) + i // RING)
                    w = (w_g, w_u, w_d)[u // 4]
                    sp.dma_start(ring[s][:, :].rearrange("p (j n) -> p j n", j=QUAD),
                                 w[bass.ds(q, 1), u % 4].rearrange("q p j n -> p (q j) n")).then_inc(landed[s], 16)

            with sp.Fori(0, QUADS) as q:
                step(q, q)
            sp.wait_ge(S["rounds"], 1)
            steps = sp.value_load(count_i[0:1, 0:1], min_val=QUADS, max_val=QUADS * ROUNDS)
            with sp.If(steps > QUADS):
                with sp.Fori(QUADS, steps) as n:
                    step(n % QUADS, n)
            with sp.Else():
                pass
            for j, parts in enumerate(post):
                i = PRE_UNITS + j
                s = i % RING
                if j < RING:
                    sp.wait_ge(used[s], steps * (EUNITS // RING) + i // RING)
                else:
                    sp.wait_ge(used_post[s], j // RING)
                if len(parts) == 2:
                    both = ring[s][:, :].rearrange("p (k a n) -> p k a n", k=8, a=2)
                    for a in range(2):
                        sp.dma_start(both[:, :, a], parts[a]).then_inc(landed_post[s], 16)
                else:
                    kn, n = parts[0].shape[1], parts[0].shape[2]
                    dst = ring[s][:, 0:kn * n].rearrange("p (k n) -> p k n", k=kn)
                    sp.dma_start(dst, parts[0]).then_inc(landed_post[s], 16)
            for i in range(4):
                copied(sp, ("out", i))
            sp.dma_start(out[0].rearrange("(t p) d -> p t d", p=P), ch(att, 0, TT, D)).then_inc(S["out_done"], 16)
            sp.wait_ge(S["out_done"], 16)

        @block.gpsimd
        def _(pool):
            pool.memset(pad[:, :], 0.0).then_inc(S["zeroed"], 1)

        @block.tensor
        def _(pe):
            ident, ones = C("ident"), C("ones")
            freed = []

            def tell(mm):
                if freed:
                    mm.then_inc(freed.pop(0), 1)

            def norm_sum(use, src, n=8):
                b = begin(pe, use)
                for c in range(n):
                    if c % (n // 2) == 0:
                        pe.wait_ge(S["squares"], SQUARES[use[0]] + c // (n // 2) + 1)
                    mm = pe.matmul(b[:, 0:T], ones, src[:, c * T:c * T + T], start=(c == 0), stop=(c == n - 1))
                    if c < n - 1:
                        tell(mm)
                filled(mm, use)

            def linear(use, w, m, src, kn=8, at=0, norm=None, last=True):
                b = begin(pe, use) if at == 0 else bank[PLACE[use][0]]
                for k in range(kn):
                    if norm is not None:
                        pe.wait_ge(S["normed"], NORMS[norm] + k + 1)
                    mm = pe.matmul(b[:, at:at + T], w[:, k, P * m:P * m + P], src[:, k * T:k * T + T],
                                   start=(k == 0), stop=(k == kn - 1))
                    if k < kn - 1:
                        tell(mm)
                if last:
                    filled(mm, use)

            def values(use, w, t, n0, n, src):
                b = begin(pe, use)
                for k in range(8):
                    mm = pe.matmul(b[:, 0:n], src[:, k * T + P * t:k * T + P * t + P], w[:, k, n0:n0 + n],
                                   start=(k == 0), stop=(k == 7))
                    if k < 7:
                        tell(mm)
                filled(mm, use)

            def turn(use, parts):
                b = begin(pe, use)
                for at, src in parts:
                    mm = pe.transpose(b[:, at:at + P], src, ident)
                filled(mm, use)

            def scores(use, parts):
                b = begin(pe, use)
                for at, n, lhsT, rhs, first, last in parts:
                    mm = pe.matmul(b[:, at:at + n], lhsT, rhs, start=first, stop=last)
                filled(mm, use)

            pe.wait_ge(S["const_in"], 16)
            pe.wait_ge(S["x_in"], 16)
            xtok = ch(att, 0, TT, D)
            for i in range(4):
                turn(("xT", i), [(c * T + t * P, xtok[:, t, (2 * i + c) * P:(2 * i + c + 1) * P])
                                 for c in range(2) for t in range(TT)])
            pe.wait_ge(S["lam_in"], 1)
            b = begin(pe, ("lam", 0))
            filled(pe.matmul(b[:, 0:2], ones, st[:, 100:102], start=True, stop=True), ("lam", 0))
            norm_sum(("n1", 0), sq)
            for u, use in enumerate(("ca", "cg", "q", "k")):
                w = u512(pre_unit(pe, u))
                for m in range(4):
                    linear((use, m), w, m, hT, norm="n1" if (u, m) == (0, 0) else None)
                freed.append(used[u % RING])
            w = u512(pre_unit(pe, 4))
            for t in range(TT):
                values(("v", t), w, t, 0, 512, hT)
            freed.append(used[4])
            for use in ("qn", "kn"):
                for i in range(2):
                    b = begin(pe, (use, i))
                    pe.wait_ge(S["squares"], SQUARES[use] + i + 1)
                    src = sq[:, 512 * i + (1024 if use == "kn" else 0):][:, 0:512]
                    filled(pe.matmul(b[:, :], C("blk64"), src, start=True, stop=True), (use, i))
            pe.wait_ge(S["qk_ready"], 4)
            for h in range(4):
                for c in range(2):
                    scores(("s1", 2 * h + c),
                           [(t * T, T, qko[64 * c:64 * c + 64, h * T + t * P:h * T + t * P + P],
                             qko[64 * c:64 * c + 64, (4 + h) * T:(5 + h) * T], True, True) for t in range(TT)])
            for u in range(4):
                w = u512(pre_unit(pe, 5 + u))
                for m in range(4):
                    linear(("gt", 4 * u + m), w, m, hT)
                freed.append(used[(5 + u) % RING])
            for h in range(4):
                pe.wait_ge(S["a_ready"], 2 * h + 2)
                turn(("aT1", h), [(kt * T + t * P, att[:, 1024 * h + T * t + kt * P:][:, 0:P])
                                  for t in range(TT) for kt in range(2)])
            for t in range(TT):
                copied(pe, ("v", t))
            for h in range(4):
                copied(pe, ("aT1", h))
                scores(("o1", h), [(0, T, vtok[:, 512 * kt + P * h:][:, 0:P], mrg[:, 512 * h + T * kt:][:, 0:T],
                                    kt == 0, kt == 1) for kt in range(2)])
            for i in range(2):
                b = begin(pe, ("on", i))
                pe.wait_ge(S["squares"], SQUARES["on"] + i + 1)
                filled(pe.matmul(b[:, :], ones, sq[:, 512 * i:512 * i + 512], start=True, stop=True), ("on", i))
            b = begin(pe, ("mu", 0))
            for c in range(4):
                pe.wait_ge(S["conved"], c + 1)
                mm = pe.matmul(b[:, 0:T], ones, big[:, (16 + c) * T:(17 + c) * T], start=(c == 0), stop=(c == 3))
                if c < 3:
                    tell(mm)
            filled(mm, ("mu", 0))
            norm_sum(("var", 0), sq[:, 1024:2048], 4)
            w = u1024(pre_unit(pe, 9))
            pe.wait_ge(S["conv_out"], 1)
            for m in range(8):
                linear(("co", m), w, m, big[:, 16 * T:20 * T], 4)
            freed.append(used[9 % RING])
            w = u1024(pre_unit(pe, 10))
            pe.wait_ge(S["attn_out"], 2)
            for m in range(8):
                linear(("ao", m), w, m, qko[:, 8 * T:12 * T], 4)
            freed.append(used[10 % RING])
            for u in range(2):
                w = u512(pre_unit(pe, 11 + u))
                pe.wait_ge(S["merged"], 8)
                for m in range(4):
                    linear(("wo", 4 * u + m), w, m, mrg)
                freed.append(used[(11 + u) % RING])
            norm_sum(("n2", 0), sq)
            pe.wait_ge(S["normed"], NORMS["n2"] + 8)
            wr = W("w_r").rearrange("p (k n) -> p k n", k=DC)
            for t in range(TT):
                b = begin(pe, ("rt", t))
                for k in range(DC):
                    pe.matmul(b[:, 0:36], hT[:, k * T + P * t:k * T + P * t + P], wr[:, k], start=(k == 0), stop=False)
                filled(pe.matmul(b[:, 0:36], ones, W("b_r"), start=False, stop=True), ("rt", t))
            for t in range(TT):
                for half in range(2):
                    turn(("h2t", 2 * t + half), [(c * P, hT[:, (4 * half + c) * T + t * P:][:, 0:P]) for c in range(4)])
            pe.wait_ge(S["member"], 1)
            mem = [member[:, t].rearrange("p g j -> p (g j)") for t in range(TT)]
            for use, terms in ((("pos", 0), (("before", 0),)), (("pos", 1), (("ones", 0), ("before", 1))),
                               (("cnt", 0), (("ones", 0), ("ones", 1)))):
                scores(use, [(0, NE, C(a), mem[t], i == 0, i == len(terms) - 1) for i, (a, t) in enumerate(terms)])
            assert not freed
            for i in range(4):
                copied(pe, ("h2t", i))
            for use in (("rt", 0), ("rt", 1), ("pos", 0), ("pos", 1), ("cnt", 0), ("wo", 6), ("wo", 7), ("n2", 0)):
                copied(pe, use)
            pe.wait_ge(S["rounds"], 1)
            steps = pe.value_load(count_i[0:1, 0:1], min_val=QUADS, max_val=QUADS * ROUNDS)
            pe.sem_inc(S["rows_full"], 1)
            with pe.Fori(0, steps) as n:
                pe.wait_ge(S["picked"], n * 2 + 2)
                pe.wait_ge(S["added"], n * 4 + 1)
                for t in range(TT):
                    mm = pe.transpose(bank[4][:, t * P:t * P + P], wpick[:, t].rearrange("p j s -> p (j s)"), ident)
                mm.then_inc(S["swt_full"], 1)
                for k in range(DC):
                    for t in range(TT):
                        rows = h2tok[:, t, 256 * (k // 2) + k % 2:256 * (k // 2) + k % 2 + 255:2]
                        mm = pe.matmul(bank[5 + k // 4][:, P * (k % 4):P * (k % 4) + P], rows,
                                       pick[:, t].rearrange("p j s -> p (j s)"), start=(t == 0), stop=(t == TT - 1))
                    if k % 4 == 3:
                        mm.then_inc(S["rows_full"], 1)

                def unit(u):
                    i = PRE_UNITS + u
                    pe.wait_ge(landed[i % RING], n * (16 * EUNITS // RING) + 16 * (i // RING + 1))
                    return ring[i % RING], used[i % RING]

                pe.wait_ge(S["rows"], n * 2 + 2)
                pe.wait_ge(S["hidden"], n + 1)
                for part in range(2):
                    for u in range(4):
                        slot, free = unit(4 * part + u)
                        w = slot[:, :].rearrange("p (j c n) -> p j c n", j=QUAD, c=2)
                        for c in range(2):
                            for j in range(QUAD):
                                mm = pe.matmul(bank[part][CAP * j:CAP * j + CAP, :],
                                               xeT[:, 2 * u + c, CAP * j:CAP * j + CAP], w[:, j, c],
                                               start=(u == 0 and c == 0), stop=(u == 3 and c == 1))
                        mm.then_inc(free, 1)
                pe.wait_ge(S["hidden"], n + 2)
                for k in range(4):
                    mm = pe.transpose(bank[7][:, P * k:P * k + P], hid[:, P * k:P * k + P], ident)
                mm.then_inc(S["hid_full"], 1)
                pe.wait_ge(S["hidT"], n + 1)
                pe.wait_ge(S["y_out"], n * 2 + 1)
                for u in range(4):
                    slot, free = unit(8 + u)
                    w = slot[:, :].rearrange("p (j n) -> p j n", j=QUAD)
                    for half in range(2):
                        for j in range(QUAD):
                            mm = pe.matmul(bank[2 + half][CAP * j:CAP * j + CAP, :],
                                           hidT[:, u, CAP * j:CAP * j + CAP], w[:, j, 512 * half:512 * half + 512],
                                           start=(u == 0), stop=(u == 3))
                    mm.then_inc(free, 1)
                pe.wait_ge(S["swt"], n + 1)
                pe.wait_ge(S["y_out"], n * 2 + 3)
                for m in range(DC):
                    mm = pe.matmul(bank[4 + m // 2][:, T * (m % 2):T * (m % 2) + T], y_e[:, P * m:P * m + P], swT,
                                   start=True, stop=True)
                    if m % 2:
                        mm.then_inc(S["comb_full"], 1)

            pe.wait_ge(S["experts_done"], 1)
            pe.wait_ge(S["pos_f"], 1)
            b = begin(pe, ("posb", 0))
            filled(pe.matmul(b[:, 0:T], C("ones", slice(0, 1)), st_pos[0:1, :], start=True, stop=True), ("posb", 0))
            norm_sum(("nmix", 0), sq)

            def post_free(j):
                freed.append(used_post[(PRE_UNITS + j) % RING])

            w = u512(post_unit(pe, 0))
            for m in range(4):
                linear(("pa", m), w, m, hT, norm="nmix" if m == 0 else None)
            post_free(0)
            w = u512(post_unit(pe, 1))
            for m, use in enumerate((("pa", 4), ("pa", 5), ("qb", 0), ("qb", 1))):
                linear(use, w, m, hT)
            post_free(1)
            w = u512(post_unit(pe, 2))
            for m in range(2):
                linear(("kb", m), w, m, hT)
            for t in range(TT):
                values(("vb", t), w, t, 256, 256, hT)
            post_free(2)
            w = u512(post_unit(pe, 3))
            for m in range(4):
                linear((("qc", "kc")[m // 2], m % 2), w, m, hT)
            post_free(3)
            w = post_unit(pe, 4)[:, :].rearrange("p (k a n) -> p k a n", k=8, a=2)
            for t in range(TT):
                values(("vc", t), w[:, :, 0], t, 0, 256, hT)
            for m in range(2):
                linear(("pd", m), w[:, :, 1], m, hT)
            post_free(4)
            b = begin(pe, ("f", 0))
            pe.wait_ge(S["wf_in"], 16)
            for k in range(8):
                mm = pe.matmul(b[0:4, 0:T], w_f[:, 4 * k:4 * k + 4], hT[:, k * T:k * T + T], start=(k == 0), stop=(k == 7))
                if k < 7:
                    tell(mm)
            filled(mm, ("f", 0))
            for use, last, at in (("rq", "qb", 6), ("rk", "kb", 8)):
                for m in range(2):
                    copied(pe, (last, m))
                scores((use, 0), [(0, 512, C("rot"), big[:, at * T:(at + 2) * T], True, True)])
            pe.wait_ge(S["rope"], 2)
            for h in range(4):
                r, m = slice(64 * (h % 2), 64 * (h % 2) + 64), h // 2
                scores(("sb", h), [(t * T, T, big[r, (6 + m) * T + t * P:][:, 0:P], big[r, (8 + m) * T:(9 + m) * T], True, True)
                                   for t in range(TT)])
            for use in ("qc", "kc"):
                for m in range(2):
                    copied(pe, (use, m))
            pe.wait_ge(S["c_rows"], 2)
            sel = C("sel").rearrange("p (h n) -> p h n", h=4)
            for h in range(4):
                parts = []
                for t in range(TT):
                    parts += [(t * T, T, qc_head[h][:, t * P:t * P + P], big[:, (12 + h // 2) * T:(13 + h // 2) * T], True, False),
                              (t * T, T, sel[:, h], neg_c, False, False)]
                    parts += [(t * T + P * kt, P, c_row[:, t * P:t * P + P], sel[:, h], False, kt == 1) for kt in range(2)]
                scores(("sc", h), parts)
            pe.wait_ge(S["z_pool"], 1)
            wp = W("w_pool")
            scores(("pl", 0), [(c * T, T, wp[:, c * P:c * P + P], z_pool[:, c * T:c * T + T], True, True) for c in range(2)])

            def small_attention(name, base, first_item):
                for h in range(4):
                    pe.wait_ge(S["a_ready"], first_item + h + 1)
                    turn(("aT" + name, h), [(kt * T + t * P, att[:, base + 512 * h + T * t + kt * P:][:, 0:P])
                                            for t in range(TT) for kt in range(2)])

            def heads_out(name, v0, uses_v):
                for t in range(TT):
                    copied(pe, (uses_v, t))
                for h2 in range(2):
                    b = begin(pe, ("o" + name, h2))
                    for c in range(2):
                        h = 2 * h2 + c
                        copied(pe, ("aT" + name, h))
                        for kt in range(2):
                            mm = pe.matmul(b[64 * c:64 * c + 64, 0:T], vtok[:, 512 * kt + v0 + 64 * h:][:, 0:64],
                                           sq[:, 512 * h + T * kt:][:, 0:T], start=(kt == 0), stop=(kt == 1))
                    filled(mm, ("o" + name, h2))

            small_attention("b", 0, 8)
            heads_out("b", 0, "vb")
            small_attention("c", 2048, 12)
            heads_out("c", 256, "vc")
            for u in range(2):
                w = u512(post_unit(pe, 5 + u))
                if u == 0:
                    pe.wait_ge(S["y_mix"], 4)
                    for k in ("ob", "oc"):
                        for h2 in range(2):
                            copied(pe, (k, h2))
                for m in range(4):
                    linear(("w2", 4 * u + m), w, m, mrg)
                post_free(5 + u)
            pe.wait_ge(S["mem_in"], 16)
            memtok = att[:, 2048:4096].rearrange("p (t d) -> p t d", t=TT)
            for i in range(4):
                turn(("mT", i), [(c * T + t * P, memtok[:, t, (2 * i + c) * P:(2 * i + c + 1) * P])
                                 for c in range(2) for t in range(TT)])
            norm_sum(("nxa", 0), mrg)
            norm_sum(("nmem", 0), big)
            for u in range(2):
                w = u512(post_unit(pe, 7 + u))
                for m in range(4):
                    linear(("kx", 4 * u + m), w, m, sq, norm="nmem" if (u, m) == (0, 0) else None)
                post_free(7 + u)
            for u in range(2):
                w = u512(post_unit(pe, 9 + u))
                for t in range(TT):
                    values(("vx", 2 * u + t), w, t, 0, 512, sq)
                post_free(9 + u)
            for u in range(2):
                w = u512(post_unit(pe, 11 + u))
                for m in range(4):
                    linear(("qx", 4 * u + m), w, m, hT)
                post_free(11 + u)
            for h in range(4):
                for e in range(2):
                    copied(pe, ("kx", 2 * h + e))
                    copied(pe, ("qx", 2 * h + e))
                scores(("sx", h), [(t * T, T, qko[:, (2 * h + e) * T + t * P:][:, 0:P],
                                    big[:, (8 + 2 * h + e) * T:(9 + 2 * h + e) * T], e == 0, e == 1)
                                   for t in range(TT) for e in range(2)])
            small_attention("x", 0, 16)
            for i in range(4):
                copied(pe, ("vx", i))
            for h in range(4):
                copied(pe, ("aTx", h))
                scores(("ox", h), [(e * T, T, big[:, 1024 * kt + 256 * h + P * e:][:, 0:P], sq[:, 512 * h + T * kt:][:, 0:T],
                                    kt == 0, kt == 1) for e in range(2) for kt in range(2)])
            for u in range(2):
                w = u512(post_unit(pe, 13 + u))
                if u == 0:
                    for h in range(4):
                        copied(pe, ("ox", h))
                for m in range(4):
                    linear(("xo", 4 * u + m), w, m, mrg)
                post_free(13 + u)
            norm_sum(("nffn", 0), sq)
            for i in range(11):
                w = post_unit(pe, FIRST_UP + i)[:, :].rearrange("p (k a n) -> p k a n", k=8, a=2)
                for a, use in enumerate(("ua", "ug")):
                    for m in range(2):
                        linear((use, i), w[:, :, a], m, hT, at=T * m, last=(m == 1), norm="nffn" if (i, a, m) == (0, 0, 0) else None)
                post_free(FIRST_UP + i)
            for m in range(8):
                begin(pe, ("dn", m))
            for i in range(6):
                w = u1024(post_unit(pe, FIRST_DN + i))
                for k in range(4 * i, min(4 * i + 4, FC)):
                    pe.wait_ge(S["up_act"], k // 2 + 1)
                    for m in range(8):
                        mm = pe.matmul(bank[PLACE[("dn", m)][0]][:, 0:T], w[:, k % 4, P * m:P * m + P],
                                       big[:, k * T:k * T + T], start=(k == 0), stop=(k == FC - 1))
                        if k == FC - 1:
                            filled(mm, ("dn", m))
                        else:
                            tell(mm)
                post_free(FIRST_DN + i)
            freed.clear()
            norm_sum(("nfin", 0), sq)
            pe.wait_ge(S["normed"], NORMS["nfin"] + 8)
            for t in range(TT):
                for half in range(2):
                    turn(("out", 2 * t + half), [(c * P, hT[:, (4 * half + c) * T + t * P:][:, 0:P]) for c in range(4)])

        @block.scalar
        def _(act):
            act.dma_start(ch(att, 0, TT, D), A["x"][0].rearrange("(t p) d -> p t d", p=P)).then_inc(S["x_in"], 16)
            act.dma_start(w_f[:, :].rearrange("p (k n) -> p k n", k=DC), w_in2[:, :, 2304:2308]).then_inc(S["wf_in"], 16)

            def move(use, dst, src_n, func=ACT.Copy, scale=1.0, rows=slice(0, P)):
                b = arrive(act, use)
                emptied(act.activation(dst, b[rows, 0:src_n], func, scale=scale), use)

            def square(src, dst, words):
                for i in range(2):
                    h = words // 2
                    signal(act.activation(dst[:, i * h:i * h + h], src[:, i * h:i * h + h], ACT.Square), "squares")

            def root(use):
                w, n = {u: (w, n) for u, w, n in ROOTS}[use]
                i = [u for u, _, _ in ROOTS].index(use)
                if i >= 2:
                    act.wait_ge(*[(S["normed"], 8), *((S["qk_ready"], k) for k in (1, 2, 3, 4)),
                                  (S["attn_out"], 1), (S["attn_out"], 2), (S["conv_z"], 4),
                                  *((S["normed"], k) for k in (16, 24, 32, 40, 48))][i - 2])
                b = arrive(act, use)
                emptied(act.activation(rs2[TURN[use]][:, 0:w], b[:, 0:w], ACT.Sqrt, bias=EPS, scale=1.0 / n), use)

            def exps(use, i, base, scale):
                act.wait_ge(S["s_max"], i + 1)
                s8 = 8 * (i % 8)
                for c in range(2):
                    e = att[:, base + c * T:base + c * T + T]
                    signal(act.activation(e, e, ACT.Exp, bias=st[:, s8 + 2 + c:s8 + 3 + c], scale=scale,
                                          accum_out=st[:, s8 + 4 + c:s8 + 5 + c]), "s_exp")

            for i in range(4):
                move(("xT", i), xT[:, 512 * i:512 * i + 512], 512)
            for i in range(4):
                copied(act, ("xT", i))
            square(xT, sq, DC * T)
            root(("n1", 0))
            move(("lam", 0), st[:, 102:104], 2, ACT.Exp)
            for m in range(4):
                move(("cg", m), mrg[:, m * T:m * T + T], T, ACT.Sigmoid)
            for at, use in enumerate("qk"):
                for m in range(4):
                    move((use, m), qko[:, (4 * at + m) * T:(4 * at + m + 1) * T], T)
                for m in range(4):
                    copied(act, (use, m))
                square(qko[:, 1024 * at:1024 * at + 1024], sq[:, 1024 * at:1024 * at + 1024], 1024)
            for t in range(TT):
                move(("v", t), vtok[:, 512 * t:512 * t + 512], 512)
            for use in ("qn", "kn"):
                for i in range(2):
                    root((use, i))
            for i in range(8):
                exps("s1", i, 512 * i, 0.125)
            for m in range(16):
                move(("gt", m), big[:, m * T:m * T + T], T, ACT.Sigmoid)
            for h in range(4):
                move(("aT1", h), mrg[:, 512 * h:512 * h + 512], 512)
            for h in range(4):
                move(("o1", h), qko[:, (8 + h) * T:(9 + h) * T], T)
            for h in range(4):
                copied(act, ("o1", h))
            square(qko[:, 2048:3072], sq[:, 0:1024], 1024)
            root(("on", 0))
            root(("on", 1))
            act.wait_ge(S["conv_dev"], 1)
            square(big[:, 16 * T:20 * T], sq[:, 1024:2048], 1024)
            root(("var", 0))
            act.wait_ge(S["conv_z"], 4)
            signal(act.activation(sq[:, 1024:2048], big[:, 16 * T:20 * T], ACT.Sigmoid), "conv_sig")
            for m in range(8):
                copied(act, ("wo", m))
            square(xT, sq, DC * T)
            root(("n2", 0))
            act.wait_ge(S["logits"], 1)
            signal(act.activation(g_gap, g_gap, ACT.Exp), "g_exp")
            for t in range(TT):
                for half in range(2):
                    move(("h2t", 2 * t + half), att[:, t * D + half * 512:t * D + half * 512 + 512], 512)
            act.dma_start(pos_i, A["positions_2"]).then_inc(S["pos_in"], 16)
            act.wait_ge(S["pair_gap"], 1)
            signal(act.activation(e_gap, e_gap, ACT.Exp), "e_exp")
            act.wait_ge(S["rounds"], 1)
            steps = act.value_load(count_i[0:1, 0:1], min_val=QUADS, max_val=QUADS * ROUNDS)
            act.sem_inc(S["y_out"], 1)
            with act.Fori(0, steps) as n:
                act.wait_ge(S["swt_full"], n + 1)
                act.activation(swT, bank[4][:, 0:T], ACT.Copy).then_inc(S["swt"], 1)
                for i in range(2):
                    act.wait_ge(S["rows_full"], n * 2 + i + 2)
                    act.activation(xeT[:, 4 * i:4 * i + 4].rearrange("p k s -> p (k s)"), bank[5 + i][:, :],
                                   ACT.Copy).then_inc(S["rows"], 1)
                i = PRE_UNITS + 3
                act.wait_ge(used[i % RING], n * 2 + i // RING + 1)
                act.activation(sig, bank[0][:, :], ACT.Sigmoid).then_inc(S["gate_sig"], 1)
                act.wait_ge(S["hid_full"], n + 1)
                act.activation(hidT.rearrange("p k s -> p (k s)"), bank[7][:, :], ACT.Copy).then_inc(S["hidT"], 1)
                i = PRE_UNITS + 11
                act.wait_ge(used[i % RING], n * 2 + i // RING + 1)
                for i in range(2):
                    act.activation(y_e[:, 512 * i:512 * i + 512], bank[2 + i][:, :], ACT.Copy).then_inc(S["y_out"], 1)

            act.wait_ge(S["experts_done"], 1)
            square(xT, sq, DC * T)
            root(("nmix", 0))
            act.wait_ge(S["ang"], 2)
            signal(act.activation(pad[:, 0:512], pad[:, 0:512], ACT.Sin), "trig")
            for m in range(6):
                move(("pa", m), big[:, m * T:m * T + T], T)
            for at, use in ((6, "qb"), (8, "kb")):
                for m in range(2):
                    move((use, m), big[:, (at + m) * T:(at + m + 1) * T], T)
            for t in range(TT):
                move(("vb", t), vtok[:, 512 * t:512 * t + 256], 256)
            for m in range(2):
                b = arrive(act, ("qc", m))
                signal(act.activation(qc_head[2 * m], b[:, 0:T], ACT.Copy, scale=C("eighth")[:, 0:1]), "act_step")
                emptied(act.activation(qc_head[2 * m + 1], b[:, 0:T], ACT.Copy, scale=C("eighth")[:, 1:2]), ("qc", m))
            for m in range(2):
                move(("kc", m), big[:, (12 + m) * T:(13 + m) * T], T)
            for t in range(TT):
                move(("vc", t), vtok[:, 512 * t + 256:512 * t + 512], 256)
            act.wait_ge(S["rows_zero"], 1)
            for m in range(2):
                move(("pd", m), pool_x[:, m, 16:16 + T], T)
            act.wait_ge(S["f_abs"], 1)
            signal(act.activation(f_e, f_abs, ACT.Exp, scale=-1.0), "f_exp")
            act.wait_ge(S["f_exp"], 1)
            signal(act.activation(f_e, f_e, ACT.Ln, bias=1.0), "f_exp")
            for i in range(4):
                exps("sb", 8 + i, 512 * i, 0.125)
            for i in range(4):
                exps("sc", 12 + i, 2048 + 512 * i, 1.0)
            for name, at in (("b", 2), ("c", 4)):
                for h in range(4):
                    move(("aT" + name, h), sq[:, 512 * h:512 * h + 512], 512)
                for h2 in range(2):
                    move(("o" + name, h2), mrg[:, (at + h2) * T:(at + h2 + 1) * T], T)
            act.dma_start(att[:, 2048:4096].rearrange("p (t d) -> p t d", t=TT),
                          A["mem_2"][0].rearrange("(t p) d -> p t d", p=P)).then_inc(S["mem_in"], 16)
            for i in range(4):
                move(("mT", i), sq[:, 512 * i:512 * i + 512], 512)
            for m in range(8):
                copied(act, ("w2", m))
            square(xT, mrg, DC * T)
            root(("nxa", 0))
            for i in range(4):
                copied(act, ("mT", i))
            square(sq, big, DC * T)
            root(("nmem", 0))
            for m in range(8):
                move(("kx", m), big[:, (8 + m) * T:(9 + m) * T], T)
            for u in range(2):
                for t in range(TT):
                    move(("vx", 2 * u + t), big[:, t * 1024 + u * 512:t * 1024 + u * 512 + 512], 512)
            for m in range(8):
                move(("qx", m), qko[:, m * T:m * T + T], T)
            for i in range(4):
                exps("sx", 16 + i, 512 * i, 1.0 / 16)
            for h in range(4):
                move(("aTx", h), sq[:, 512 * h:512 * h + 512], 512)
            for h in range(4):
                move(("ox", h), mrg[:, 512 * h:512 * h + 512], 512)
            for m in range(8):
                copied(act, ("xo", m))
            square(xT, sq, DC * T)
            root(("nffn", 0))
            act.wait_ge(S["pads_zero"], 1)
            for i in range(11):
                if i:
                    act.wait_ge(S["up_conv"], i)
                for a, use in enumerate(("ua", "ug")):
                    b = arrive(act, (use, i))
                    emptied(act.activation(up_x[:, 2 * a:2 * a + 2, 2:2 + T], b[:, :].rearrange("p (c t) -> p c t", c=2),
                                           ACT.Copy), (use, i))
                act.wait_ge(S["up_conv"], i + 1)
                signal(act.activation(up_s, up_y[:, 512:1024], ACT.Sigmoid), "up_sig")
            for m in range(8):
                copied(act, ("dn", m))
            square(xT, sq, DC * T)
            root(("nfin", 0))
            for i in range(4):
                move(("out", i), att[:, 512 * i:512 * i + 512], 512)

        @block.vector
        def _(dve):
            def step(ins):
                done(dve, ins, "dve_step")

            def inverse_root(use):
                w = {u: w for u, w, _ in ROOTS}[use]
                copied(dve, use)
                r = rs2[TURN[use]][:, 0:w]
                step(dve.reciprocal(r, r))
                return r

            def normalise(use, g, src, dst):
                r = inverse_root(use)
                for c in range(DC):
                    signal(dve.scalar_tensor_tensor(out=dst[:, c * T:c * T + T], in0=src[:, c * T:c * T + T],
                                                    scalar=col(g, c), in1=r, op0=ALU.mult, op1=ALU.mult), "normed")

            def maxima(use, i, base, scale, mask=None):
                b = arrive(dve, use)
                s = att[:, base:base + 512]
                if mask is None:
                    ins = dve.tensor_copy(s, b[:, :])
                else:
                    ins = dve.tensor_tensor(s, b[:, :], C(mask), ALU.add)
                emptied(ins, use)
                copied(dve, use)
                s8 = 8 * (i % 8)
                step(dve.tensor_reduce(st[:, s8:s8 + 2], s.rearrange("p (t k) -> p t k", t=TT), AX, ALU.max))
                signal(dve.tensor_scalar(st[:, s8 + 2:s8 + 4], st[:, s8:s8 + 2], -scale, None, ALU.mult), "s_max")

            def shares(i, base, mult=None):
                dve.wait_ge(S["s_exp"], 2 * i + 2)
                s8 = 8 * (i % 8)
                s = att[:, base:base + 512].rearrange("p (t k) -> p t k", t=TT)
                if mult is not None:
                    step(dve.tensor_tensor(s, s, C(mult).rearrange("p (t k) -> p t k", t=TT), ALU.mult))
                    step(dve.tensor_reduce(st[:, s8 + 4:s8 + 6], s, AX, ALU.add))
                step(dve.reciprocal(st[:, s8 + 6:s8 + 8], st[:, s8 + 4:s8 + 6]))
                signal(dve.tensor_tensor(s, s, st[:, s8 + 6:s8 + 8].unsqueeze(2).broadcast_to([P, TT, T]), ALU.mult), "a_ready")

            dve.wait_ge(S["const_in"], 16)
            dve.wait_ge(S["par_in"], 16)
            step(dve.memset(st[:, :], 0.0))
            step(dve.tensor_tensor(st[:, 98:99], W("lam_q"), W("lam_k"), ALU.mult))
            signal(dve.tensor_scalar(st[:, 100:102], C("halves"), st[:, 98:99], None, ALU.mult), "lam_in")
            copied(dve, ("lam", 0))
            step(dve.tensor_tensor(st[:, 104:105], st[:, 103:104], st[:, 102:103], ALU.subtract))
            step(dve.tensor_scalar(st[:, 104:105], st[:, 104:105], -LAM0, None, ALU.add))
            step(dve.tensor_scalar(st[:, 105:106], W("sub_g"), 1.0 - LAM0, None, ALU.mult))
            for i in range(4):
                copied(dve, ("xT", i))
            normalise(("n1", 0), "g1", xT, hT)
            dve.wait_ge(S["zeroed"], 1)
            rows = pad[:, :].rearrange("p (c t) -> p c t", c=4)
            for m in range(4):
                b = arrive(dve, ("ca", m))
                copied(dve, ("cg", m))
                emptied(dve.tensor_tensor(rows[:, m, CW - 1:], b[:, 0:T], mrg[:, m * T:m * T + T], ALU.mult), ("ca", m))
            for at, use in enumerate(("qn", "kn")):
                for i in range(2):
                    r = inverse_root((use, i))
                    x = qko[:, 1024 * at + 512 * i:1024 * at + 512 * i + 512]
                    signal(dve.scalar_tensor_tensor(out=x, in0=x, scalar=col(("q_g", "k_g")[at], 0), in1=r,
                                                    op0=ALU.mult, op1=ALU.mult), "qk_ready")
            for i in range(8):
                maxima(("s1", i), i, 512 * i, 0.125, "causal")
            for h in range(4):
                dve.wait_ge(S["s_exp"], 4 * h + 4)
                s0, s1 = 16 * h, 16 * h + 8
                step(dve.reciprocal(st[:, s0 + 6:s0 + 8], st[:, s0 + 4:s0 + 6]))
                step(dve.reciprocal(st[:, s1 + 6:s1 + 8], st[:, s1 + 4:s1 + 6]))
                for t in range(TT):
                    e0, e1 = (att[:, 1024 * h + 512 * c + T * t:][:, 0:T] for c in range(2))
                    step(dve.tensor_scalar(e1, e1, st[:, s1 + 6 + t:s1 + 7 + t], st[:, 104:105], ALU.mult, ALU.mult))
                    signal(dve.scalar_tensor_tensor(out=e0, in0=e0, scalar=st[:, s0 + 6 + t:s0 + 7 + t], in1=e1,
                                                    op0=ALU.mult, op1=ALU.add), "a_ready")
            for m in range(4):
                copied(dve, ("ca", m))
            for m in range(4):
                y = big[:, (16 + m) * T:(17 + m) * T]
                step(dve.tensor_scalar(y, rows[:, m, 0:T], col("taps", CW * m), col("conv_b", m), ALU.mult, ALU.add))
                for j in range(1, CW):
                    ins = dve.scalar_tensor_tensor(out=y, in0=rows[:, m, j:j + T], scalar=col("taps", CW * m + j), in1=y,
                                                   op0=ALU.mult, op1=ALU.add)
                    if j < CW - 1:
                        step(ins)
                    else:
                        signal(ins, "conved")
            for i in range(2):
                r = inverse_root(("on", i))
                x = qko[:, 2048 + 512 * i:2560 + 512 * i]
                for h in range(2):
                    copied(dve, ("o1", 2 * i + h))
                signal(dve.scalar_tensor_tensor(out=x, in0=x, scalar=st[:, 105:106], in1=r,
                                                op0=ALU.mult, op1=ALU.mult), "attn_out")
            y4 = big[:, 16 * T:20 * T].rearrange("p (c t) -> p c t", c=4)
            b = arrive(dve, ("mu", 0))
            emptied(dve.tensor_scalar(hT[:, 0:T], b[:, 0:T], 1.0 / 512, None, ALU.mult), ("mu", 0))
            copied(dve, ("mu", 0))
            dve.wait_ge(S["conved"], 4)
            signal(dve.tensor_tensor(y4, y4, hT[:, 0:T].unsqueeze(1).broadcast_to([P, 4, T]), ALU.subtract), "conv_dev")
            r = inverse_root(("var", 0))
            dve.wait_ge(S["conv_dev"], 1)
            step(dve.tensor_tensor(y4, y4, r.unsqueeze(1).broadcast_to([P, 4, T]), ALU.mult))
            for m in range(4):
                signal(dve.tensor_scalar(y4[:, m], y4[:, m], col("ln_g", m), col("ln_b", m), ALU.mult, ALU.add), "conv_z")
            dve.wait_ge(S["conv_z"], 4)
            dve.wait_ge(S["conv_sig"], 1)
            signal(dve.tensor_tensor(big[:, 16 * T:20 * T], big[:, 16 * T:20 * T], sq[:, 1024:2048], ALU.mult), "conv_out")
            for m in range(8):
                b = arrive(dve, ("co", m))
                copied(dve, ("gt", m))
                emptied(dve.tensor_tensor(mrg[:, m * T:m * T + T], b[:, 0:T], big[:, m * T:m * T + T], ALU.mult), ("co", m))
            for m in range(8):
                b = arrive(dve, ("ao", m))
                copied(dve, ("gt", 8 + m))
                g = big[:, (8 + m) * T:(9 + m) * T]
                emptied(dve.tensor_tensor(g, b[:, 0:T], g, ALU.mult), ("ao", m))
                copied(dve, ("ao", m))
                copied(dve, ("co", m))
                y = mrg[:, m * T:m * T + T]
                signal(dve.tensor_tensor(y, y, g, ALU.add), "merged")

            def residual(use, n=8):
                for m in range(n):
                    b = arrive(dve, (use, m))
                    x = xT[:, m * T:m * T + T]
                    emptied(dve.tensor_tensor(x, b[:, 0:T], x, ALU.add), (use, m))
                for m in range(n):
                    copied(dve, (use, m))

            residual("wo")
            normalise(("n2", 0), "g2", xT, hT)
            for t in range(TT):
                b = arrive(dve, ("rt", t))
                emptied(dve.tensor_copy(logit[:, t], b[:, 0:36]), ("rt", t))
            for t in range(TT):
                copied(dve, ("rt", t))
            lg = logit[:, :, 0:NG]
            le = logit[:, :, NG:36].rearrange("p t (g j) -> p t g j", g=NG)

            def first_max(values, n, best, one_hot, tmp):
                fall = C("falling")[:, 0:n].unsqueeze(1).broadcast_to([P, TT, n])
                step(dve.tensor_reduce(best, values, AX, ALU.max))
                step(dve.tensor_tensor(tmp, values, best.unsqueeze(2).broadcast_to([P, TT, n]), ALU.is_equal))
                step(dve.tensor_tensor(tmp, tmp, fall, ALU.mult))
                step(dve.tensor_reduce(tie, tmp, AX, ALU.max))
                step(dve.tensor_tensor(one_hot, tmp, tie.unsqueeze(2).broadcast_to([P, TT, n]), ALU.is_equal))

            first_max(lg, NG, g_max, g_hot, g_tmp)
            signal(dve.tensor_tensor(g_gap3, lg, g_max.unsqueeze(2).broadcast_to([P, TT, NG]), ALU.subtract), "logits")
            hot4 = g_hot.unsqueeze(3).broadcast_to([P, TT, NG, EG])
            for t in range(TT):
                step(dve.tensor_tensor(e_all[:, t], le[:, t], hot4[:, t], ALU.mult))
            step(dve.tensor_reduce(e_val, e_all.rearrange("p t g j -> p t j g"), AX, ALU.add))
            first_max(e_val, EG, e_max1, hot1, e_tmp)
            step(dve.scalar_tensor_tensor(out=e_val, in0=hot1, scalar=-BIG, in1=e_val, op0=ALU.mult, op1=ALU.add))
            first_max(e_val, EG, e_max2, hot2, e_tmp)
            signal(dve.tensor_tensor(e_gap, e_max2, e_max1, ALU.subtract), "pair_gap")
            step(dve.tensor_tensor(e_tmp, hot1, hot2, ALU.add))
            for t in range(TT):
                step(dve.tensor_tensor(member[:, t], hot4[:, t], e_tmp[:, t].unsqueeze(1).broadcast_to([P, NG, EG]), ALU.mult))
            signal(dve.memset(tie, 0.0), "member")
            dve.wait_ge(S["g_exp"], 1)
            step(dve.tensor_reduce(g_sum, g_gap3, AX, ALU.add))
            dve.wait_ge(S["e_exp"], 1)
            step(dve.scalar_tensor_tensor(out=g_sum, in0=e_gap, scalar=1.0, in1=g_sum, op0=ALU.add, op1=ALU.mult))
            step(dve.reciprocal(w_1, g_sum))
            step(dve.tensor_tensor(w_2, w_1, e_gap, ALU.mult))
            step(dve.tensor_tensor(hot1, hot1, w_1.unsqueeze(2).broadcast_to([P, TT, EG]), ALU.mult))
            step(dve.tensor_tensor(hot2, hot2, w_2.unsqueeze(2).broadcast_to([P, TT, EG]), ALU.mult))
            step(dve.tensor_tensor(hot1, hot1, hot2, ALU.add))
            for t in range(TT):
                step(dve.tensor_tensor(e_all[:, t], hot4[:, t], hot1[:, t].unsqueeze(1).broadcast_to([P, NG, EG]), ALU.mult))
            for t in range(TT):
                b = arrive(dve, ("pos", t))
                mt = member[:, t].rearrange("p g j -> p (g j)")
                q = place_of[:, t]
                emptied(dve.scalar_tensor_tensor(out=q, in0=b[:, 0:NE], scalar=1.0, in1=mt, op0=ALU.add, op1=ALU.mult), ("pos", t))
                copied(dve, ("pos", t))
                step(dve.tensor_scalar(q, q, -1.0, None, ALU.add))
                so = slot_of[:, t].rearrange("p (r e) -> p r e", r=ROUNDS)
                step(dve.tensor_tensor(so, q.unsqueeze(1).broadcast_to([P, ROUNDS, NE]),
                                       C("round_start").unsqueeze(2).broadcast_to([P, ROUNDS, NE]), ALU.subtract))
                wo = weight_of[:, t].rearrange("p (r e) -> p r e", r=ROUNDS)
                step(dve.tensor_copy(wo, e_all[:, t].rearrange("p g j -> p (g j)").unsqueeze(1).broadcast_to([P, ROUNDS, NE])))
            b = arrive(dve, ("cnt", 0))
            emptied(dve.tensor_reduce(st[:, 106:107], b[:, 0:NE], AX, ALU.max), ("cnt", 0))
            copied(dve, ("cnt", 0))
            step(dve.tensor_tensor(st[:, 108:116], st[:, 106:107].broadcast_to([P, ROUNDS]), C("round_start"), ALU.is_gt))
            step(dve.tensor_reduce(st[:, 107:108], st[:, 108:116], AX, ALU.add))
            signal(dve.tensor_scalar(count_i[:, :], st[:, 107:108], float(QUADS), None, ALU.mult), "rounds")
            dve.wait_ge(S["rounds"], 1)
            steps = dve.value_load(count_i[0:1, 0:1], min_val=QUADS, max_val=QUADS * ROUNDS)
            iota = C("iota").unsqueeze(1).broadcast_to([P, QUAD, CAP])
            dve.sem_inc(S["hidden"], 1)
            dve.sem_inc(S["added"], 1)
            with dve.Fori(0, steps) as n:
                dve.wait_ge(S["rows_full"], n * 2 + 1)
                dve.wait_ge(S["added"], n * 4 + 1)
                for t in range(TT):
                    here = slot_of[:, t, bass.ds(n * QUAD, QUAD)].unsqueeze(2).broadcast_to([P, QUAD, CAP])
                    dve.tensor_tensor(pick[:, t], here, iota, ALU.is_equal).then_inc(S["pick_step"], 1)
                dve.wait_ge(S["pick_step"], n * 2 + 2)
                for t in range(TT):
                    wt = weight_of[:, t, bass.ds(n * QUAD, QUAD)].unsqueeze(2).broadcast_to([P, QUAD, CAP])
                    dve.tensor_tensor(wpick[:, t], pick[:, t], wt, ALU.mult).then_inc(S["picked"], 1)
                dve.wait_ge(S["gate_sig"], n + 1)
                dve.tensor_tensor(sig, bank[0][:, :], sig, ALU.mult).then_inc(S["hid_step"], 1)
                dve.wait_ge(S["hid_step"], n + 1)
                i = PRE_UNITS + 7
                dve.wait_ge(used[i % RING], n * 2 + i // RING + 1)
                dve.tensor_tensor(hid, bank[1][:, :], sig, ALU.mult).then_inc(S["hidden"], 1)
                for i in range(4):
                    dve.wait_ge(S["comb_full"], n * 4 + i + 1)
                    x = xT[:, 512 * i:512 * i + 512]
                    dve.tensor_tensor(x, bank[4 + i][:, :], x, ALU.add).then_inc(S["added"], 1)

            done(dve, dve.memset(st[:, :], 0.0), "experts_done")
            dve.wait_ge(S["pos_in"], 16)
            signal(dve.tensor_copy(st_pos[0:1, :], pos_i), "pos_f")
            b = arrive(dve, ("posb", 0))
            ang, turns = att[:, 2048:2048 + T], att[:, 2304:2304 + T]
            emptied(dve.tensor_scalar(ang, b[:, 0:T], C("inv_freq"), None, ALU.mult), ("posb", 0))
            copied(dve, ("posb", 0))
            step(dve.tensor_scalar(turns, ang, 1.0 / (2 * np.pi), None, ALU.mult))
            step(dve.tensor_scalar(turns, turns, MAGIC, None, ALU.add))
            step(dve.tensor_scalar(turns, turns, -MAGIC, None, ALU.add))
            for part in TWO_PI:
                step(dve.scalar_tensor_tensor(out=ang, in0=turns, scalar=-part, in1=ang, op0=ALU.mult, op1=ALU.add))
            lim = 3.1415925
            signal(dve.tensor_scalar(pad[:, T:2 * T], ang, lim, -lim, ALU.min, ALU.max), "ang")
            step(dve.tensor_scalar(ang, ang, np.pi / 2, None, ALU.add))
            step(dve.tensor_scalar(turns, ang, lim, -2 * np.pi, ALU.is_gt, ALU.mult))
            step(dve.tensor_tensor(ang, ang, turns, ALU.add))
            signal(dve.tensor_scalar(pad[:, 0:T], ang, lim, -lim, ALU.min, ALU.max), "ang")
            normalise(("nmix", 0), "g_mix", xT, hT)
            step(dve.memset(pool_x, 0.0))
            step(dve.memset(conv_x, 0.0))
            step(dve.memset(c_rows, 0.0))
            signal(dve.memset(f_zero, 0.0), "rows_zero")
            for m in range(6):
                copied(dve, ("pa", m))
            step(dve.tensor_tensor(conv_x[:, :, 2:], ch(big, 4, 2), ch(big, 0, 2), ALU.mult))
            for c in range(2):
                y = mrg[:, c * T:c * T + T]
                step(dve.tensor_scalar(y, conv_x[:, c, 0:T], col("w_sc", 3 * c), None, ALU.mult))
                for j in range(1, 3):
                    step(dve.scalar_tensor_tensor(out=y, in0=conv_x[:, c, j:j + T], scalar=col("w_sc", 3 * c + j), in1=y,
                                                  op0=ALU.mult, op1=ALU.add))
                signal(dve.tensor_tensor(y, y, ch(big, 2 + c), ALU.mult), "y_mix")
            b = arrive(dve, ("f", 0))
            emptied(dve.tensor_scalar(f_z, b[0:4, 0:T], col("b_f", 0, slice(0, 4)), None, ALU.add), ("f", 0))
            copied(dve, ("f", 0))
            step(dve.tensor_scalar(f_abs, f_z, -1.0, None, ALU.mult))
            signal(dve.tensor_tensor(f_abs, f_abs, f_z, ALU.max), "f_abs")
            step(dve.tensor_scalar(f_z, f_z, 0.0, None, ALU.min))
            dve.wait_ge(S["trig"], 1)
            for use, at in (("rq", 6), ("rk", 8)):
                b = arrive(dve, (use, 0))
                x = ch(big, at, 2)
                cos = pad[:, 0:T].unsqueeze(1).broadcast_to([P, 2, T])
                sin = pad[:, T:2 * T].unsqueeze(1).broadcast_to([P, 2, T])
                r3 = rs2[1][:, :].rearrange("p (c t) -> p c t", c=2)
                emptied(dve.tensor_tensor(r3, b[:, :].rearrange("p (c t) -> p c t", c=2), sin, ALU.mult), (use, 0))
                copied(dve, (use, 0))
                step(dve.tensor_tensor(x, x, cos, ALU.mult))
                done(dve, dve.tensor_tensor(x, x, r3, ALU.add), "rope")
            dve.wait_ge(S["f_exp"], 2)
            step(dve.tensor_tensor(f_z, f_z, f_e, ALU.subtract))
            signal(dve.tensor_tensor_scan(c_row[0:4], f_z, f_zero, 0.0, ALU.add, ALU.add), "c_rows")
            dve.wait_ge(S["c_rows"], 1)
            signal(dve.tensor_scalar(neg_c[0:4], c_row[0:4], -1.0, None, ALU.mult), "c_rows")
            for m in range(2):
                copied(dve, ("pd", m))
            width = 16 + T
            step(dve.tensor_copy(pool_s[0][:, :, 0:1], pool_x[:, :, 0:1]))
            step(dve.tensor_tensor(pool_s[0][:, :, 1:], pool_x[:, :, 1:], pool_x[:, :, :width - 1], ALU.add))
            step(dve.tensor_copy(pool_s[1][:, :, 0:2], pool_s[0][:, :, 0:2]))
            step(dve.tensor_tensor(pool_s[1][:, :, 2:], pool_s[0][:, :, 2:], pool_s[0][:, :, :width - 2], ALU.add))
            z = z_pool.rearrange("p (c t) -> p c t", c=2)
            step(dve.tensor_copy(z[0:64, 0], pool_s[0][0:64, 0, 16:]))
            step(dve.tensor_copy(z[64:128, 0], pool_s[1][64:128, 0, 16:]))
            a8, a16 = pool_s[0][:, 1], pool_s[0][:, 0]
            step(dve.tensor_copy(a8[:, 0:4], pool_s[1][:, 1, 0:4]))
            step(dve.tensor_tensor(a8[:, 4:], pool_s[1][:, 1, 4:], pool_s[1][:, 1, :width - 4], ALU.add))
            step(dve.tensor_tensor(a16[:, 8:], a8[:, 8:], a8[:, :width - 8], ALU.add))
            step(dve.tensor_copy(z[0:64, 1], a8[0:64, 16:]))
            step(dve.tensor_copy(z[64:128, 1], a16[64:128, 16:]))
            step(dve.tensor_tensor(z_pool, z_pool, C("inv_count"), ALU.mult))
            signal(dve.tensor_tensor(z, z, pool_x[:, :, 16:], ALU.subtract), "z_pool")
            for i in range(4):
                maxima(("sb", i), 8 + i, 512 * i, 0.125, "dil_mask")
            for i in range(4):
                maxima(("sc", i), 12 + i, 2048 + 512 * i, 1.0, "causal")
            for i in range(4):
                shares(8 + i, 512 * i, "dil_mult")
            for i in range(4):
                shares(12 + i, 2048 + 512 * i)
            b = arrive(dve, ("pl", 0))
            signal(dve.tensor_scalar(mrg[:, 6 * T:7 * T], b[:, 0:T], col("pool_g", 0), None, ALU.mult), "y_mix")
            emptied(dve.tensor_scalar(mrg[:, 7 * T:8 * T], b[:, T:2 * T], col("pool_g", 1), None, ALU.mult), ("pl", 0))
            copied(dve, ("pl", 0))
            signal(dve.memset(st[:, 120:121], 0.0), "y_mix")
            residual("w2")
            normalise(("nxa", 0), "g_xa", xT, hT)
            for i in range(4):
                copied(dve, ("mT", i))
            normalise(("nmem", 0), "g_mem", sq, sq)
            for i in range(4):
                maxima(("sx", i), 16 + i, 512 * i, 1.0 / 16)
            for i in range(4):
                shares(16 + i, 512 * i)
            residual("xo")
            signal(dve.memset(pad[:, :], 0.0), "pads_zero")
            normalise(("nffn", 0), "g_ffn", xT, hT)
            for i in range(11):
                for a, use in enumerate(("ua", "ug")):
                    copied(dve, (use, i))
                for q in range(4):
                    chunk = 2 * i + q % 2 + FC * (q // 2)
                    y = up_y[:, q * T:q * T + T]
                    step(dve.tensor_scalar(y, up_x[:, q, 0:T], col("ff_taps", 3 * chunk), None, ALU.mult))
                    for j in range(1, 3):
                        ins = dve.scalar_tensor_tensor(out=y, in0=up_x[:, q, j:j + T], scalar=col("ff_taps", 3 * chunk + j),
                                                       in1=y, op0=ALU.mult, op1=ALU.add)
                        if q == 3 and j == 2:
                            done(dve, ins, "up_conv")
                        else:
                            step(ins)
                step(dve.tensor_tensor(up_y[:, 0:512], up_y[:, 0:512], up_y[:, 512:1024], ALU.mult))
                dve.wait_ge(S["up_sig"], i + 1)
                done(dve, dve.tensor_tensor(big[:, 2 * i * T:(2 * i + 2) * T], up_y[:, 0:512], up_s, ALU.mult), "up_act")
            residual("dn")
            normalise(("nfin", 0), "g_fin", xT, hT)


WEIGHTS = ["x", "w_in", "w_conv_out", "w_attn_out", "w_out", "w_gate_e", "w_up_e", "w_down_e", "mem_2", "positions_2",
           "w_in_2", "w_out_2", "w_xq_2", "w_xkv_2", "w_xo_2", "w_up_2", "w_down_2"]


def lay_out(inputs):
    at, n = param_places()
    par = np.zeros((P, n), np.float32)

    def put(name, a, rows=P):
        i, j = at[name]
        par[0:rows, i:j] = a

    def cols(a):
        return np.asarray(a).reshape(-1, P).T

    for name, key in (("g1", "attn_norm_g"), ("conv_b", "conv_dw_b"), ("ln_g", "conv_ln_g"), ("ln_b", "conv_ln_b"),
                      ("sub_g", "subln_g"), ("g2", "ffn_norm_g"), ("g_mix", "g_mix_2"), ("pool_g", "pool_scale_2"),
                      ("g_xa", "g_xa_2"), ("g_mem", "g_mem_2"), ("g_ffn", "g_ffn_2"), ("g_fin", "g_final_2")):
        put(name, cols(inputs[key]))

    def taps(a):
        a = np.asarray(a)[0]
        return a.reshape(a.shape[0], -1, P).transpose(2, 1, 0).reshape(P, -1)

    put("taps", taps(inputs["conv_dw_w"]))
    put("w_sc", taps(inputs["w_sconv_2"]))
    put("ff_taps", taps(inputs["w_ffconv_2"]))
    for name, keys in (("q_g", ("q_norm_g", "q_norm_g")), ("k_g", ("k_norm_g", "k_norm_g")),
                       ("lam_q", ("lambda_q1", "lambda_q2")), ("lam_k", ("lambda_k1", "lambda_k2"))):
        put(name, np.concatenate([np.asarray(inputs[k])[0] for k in keys]).reshape(P, 1))
    w_r = np.concatenate([np.asarray(inputs["w_router_group"])[0], np.asarray(inputs["w_router_expert"])[0]], 1)
    put("w_r", w_r.reshape(DC, P, 36).transpose(1, 0, 2).reshape(P, -1))
    put("b_r", np.concatenate([np.asarray(inputs["b_router_group"])[0], np.asarray(inputs["b_router_expert"])[0]]).reshape(1, 36), 1)
    put("b_f", np.asarray(inputs["b_forget_2"]).reshape(4, 1), 4)
    w = np.asarray(inputs["w_pool_2"])[0]
    i, _ = at["w_pool"]
    for g in range(4):
        h = 64 * (g % 2)
        par[h:h + 64, i + P * (g // 2) + h:i + P * (g // 2) + h + 64] = w[g]
    return par


def kernel(**inputs):
    import concourse.bacc as bacc
    from concourse.bass_utils import run_bass_kernel_spmd

    nc = bacc.Bacc("TRN2", target_bir_lowering=False, num_devices=1)
    const, places = constants()
    arrays = {"const": const, "par": lay_out(inputs)}
    for name in WEIGHTS:
        arrays[name] = np.ascontiguousarray(inputs[name])
    A = {name: nc.dram_tensor(f"in_{name}_dram", a.shape, mybir.dt.from_np(a.dtype), kind="ExternalInput").ap()
         for name, a in arrays.items()}
    out = nc.dram_tensor("out_0_dram", (1, T, D), F32, kind="ExternalOutput").ap()
    two_blocks_kernel(nc, A, out, places)
    r = run_bass_kernel_spmd(nc, [{f"in_{name}_dram": a for name, a in arrays.items()}], core_ids=[0])
    return r.results[0]["out_0_dram"]
```

```python
from contextlib import ExitStack

import numpy as np
import concourse.bass as bass
from concourse import mybir

F32 = mybir.dt.float32
F32R = mybir.dt.float32r
I32 = mybir.dt.int32
ALU = mybir.AluOpType
ACT = mybir.ActivationFunctionType
AX = mybir.AxisListType.X

P = 128
T = 256
D = 1024
DC = D // P
TT = T // P
CW = 31
NE, NG, EG = 32, 4, 8
CAP = 32
QUAD = P // CAP
QUADS = NE // QUAD
ROUNDS = T // CAP
FF = 2816
FC = FF // P
RING = 6
UW = DC * 512
EUNITS = 12
EPS = 1e-6
BIG = 1e30
PRE_UNITS = 6
POOLS = (2, 4, 8, 16)
LAM0 = 0.2
MAGIC = 12582912.0
TWO_PI = (6.28125, 0.0019340515136718750, 2 * np.pi - 6.28125 - 0.0019340515136718750)


def constants():
    cols, at, n = [], {}, 0

    def add(name, a):
        nonlocal n
        a = np.asarray(a, np.float32).reshape(P, -1)
        at[name] = (n, n + a.shape[1])
        cols.append(a)
        n += a.shape[1]

    p = np.arange(P)
    add("ident", np.eye(P))
    add("ones", np.ones((P, P)))
    add("blk64", p[:, None] // 64 == p[None, :] // 64)
    add("before", p[:, None] < p[None, :])
    rot = np.zeros((P, P))
    for m in range(P):
        if m % 64 < 8:
            rot[m + 8, m] = -1.0
        elif m % 64 < 16:
            rot[m - 8, m] = 1.0
    add("rot", rot)
    d = (np.arange(TT)[None, :, None] * P + p[:, None, None]) - np.arange(T)[None, None, :]
    add("causal", np.where(d >= 0, 0.0, -BIG))
    mult = sum(((d >= 0) & (d % dil == 0) & (d <= w)).astype(np.float32) for w, dil in ((128, 1), (512, 4), (2048, 16)))
    add("dil_mask", np.where(mult > 0, 0.0, -BIG))
    add("dil_mult", mult)
    w = np.array([[POOLS[2 * c + (q >= 64)] for c in range(2)] for q in p])
    add("inv_count", 1.0 / np.minimum(np.arange(T)[None, None, :] + 1, w[:, :, None]))
    sel = np.zeros((P, 4, P))
    for h in range(4):
        sel[h, h, :] = 1.0
    add("sel", sel)
    f = np.float32(500000.0) ** (-np.arange(0, 16, 2, dtype=np.float32) / np.float32(16))
    add("inv_freq", [f[q % 8] if q % 64 < 16 else 0.0 for q in p])
    add("iota", np.tile(np.arange(CAP), (P, 1)))
    add("round_start", np.tile(np.arange(ROUNDS) * CAP, (P, 1)))
    add("falling", np.tile(8.0 - np.arange(8), (P, 1)))
    add("halves", np.stack([p < 64, p >= 64], 1))
    add("eighth", np.stack([p < 64, p >= 64], 1) / 8.0)
    add("neg_half", np.full((P, 1), -0.5))
    return np.concatenate(cols, 1), at


PARAMS = [("g1", 8), ("taps", 4 * CW), ("conv_b", 4), ("ln_g", 4), ("ln_b", 4), ("q_g", 1), ("k_g", 1), ("sub_g", 1),
          ("g2", 8), ("w_r", DC * 36), ("b_r", 36), ("lam_q", 1), ("lam_k", 1), ("g_mix", 8), ("b_f", 1), ("w_sc", 6),
          ("w_pool", 256), ("pool_g", 2), ("g_xa", 8), ("g_mem", 8), ("g_ffn", 8), ("ff_taps", 2 * FC * 3), ("g_fin", 8)]


def param_places():
    at, n = {}, 0
    for name, w in PARAMS:
        at[name] = (n, n + w)
        n += w
    return at, n


def psum_plan():
    def some(name, a, b):
        return [(name, i) for i in range(a, b)]

    uses = some("xT", 0, 4) + [("lam", 0), ("n1", 0)]
    uses += some("ca", 0, 4) + some("cg", 0, 4) + some("q", 0, 4) + some("k", 0, 4) + some("v", 0, 2)
    uses += some("qn", 0, 2) + some("kn", 0, 2) + some("gt", 0, 8) + some("s1", 0, 4)
    uses += [("mu", 0)] + some("s1", 4, 8) + some("gt", 8, 12) + [("var", 0)] + some("gt", 12, 16) + some("co", 0, 8) + some("aT1", 0, 4) + some("o1", 0, 4) + some("on", 0, 2)
    uses += some("mT", 0, 4) + some("ao", 0, 8) + some("wo", 0, 4) + [("nmem", 0)] + some("wo", 4, 8)
    uses += some("kx", 0, 2) + [("n2", 0)] + some("kx", 2, 4) + some("rt", 0, 2) + some("h2t", 0, 4) + some("kx", 4, 8)
    uses += some("pos", 0, 2) + [("cnt", 0)]
    uses += [("posb", 0), ("nmix", 0)] + some("vx", 0, 2) + some("pa", 4, 6) + some("qb", 0, 2) + some("kb", 0, 2)
    uses += some("vb", 0, 2) + [("rq", 0), ("rk", 0)] + some("qc", 0, 2) + some("kc", 0, 2) + [("f", 0)]
    uses += some("sb", 0, 4) + some("vx", 2, 4) + some("sc", 0, 4) + some("vc", 0, 2) + some("pd", 0, 2) + some("pa", 0, 4)
    uses += some("aTb", 0, 4) + some("ob", 0, 2) + [("pl", 0)] + some("aTc", 0, 4) + some("oc", 0, 2)
    uses += [("w2", m) for m in range(8)]
    uses += [("nxa", 0)] + some("qx", 0, 4) + some("sx", 0, 2) + some("qx", 4, 8) + some("sx", 2, 4)
    uses += [("aTx", h) for h in range(4)] + [("ox", h) for h in range(4)] + [("xo", m) for m in range(8)]
    uses += [("nffn", 0)] + [(k, i) for i in range(11) for k in ("ua", "ug")] + [("dn", m) for m in range(8)]
    uses += [("nfin", 0)] + [("out", i) for i in range(4)]
    place, turn = {}, [0] * 8
    for i, u in enumerate(uses):
        turn[i % 8] += 1
        place[u] = (i % 8, turn[i % 8])
    return place


def two_blocks_kernel(nc, A, out, CAT):
    PAT, PW = param_places()
    PLACE = psum_plan()
    CWID = max(b for _, b in CAT.values())

    with ExitStack() as ctx:
        def sb(name, words, dt=F32):
            return ctx.enter_context(nc.sbuf_tensor(name, [P, words], dt))

        def sem(name):
            return ctx.enter_context(nc.semaphore(name))

        sizes = [(f"ring{i}", UW) for i in range(RING)]
        sizes += [("hT", DC * T), ("big", FC * T), ("qko", 12 * T), ("vtok", TT * 512), ("mrg", DC * T), ("att", 16 * T)]
        with ExitStack() as first:
            tiles = {n: first.enter_context(nc.sbuf_tensor(n, [P, w], F32)) for n, w in sizes}
        parts = {n: sb(f"{n}_parts", w, F32R) for n, w in sizes}
        ring = [tiles[f"ring{i}"] for i in range(RING)]
        ring_r = [parts[f"ring{i}"] for i in range(RING)]
        hT, big, qko, vtok, mrg, att = (tiles[n] for n in ("hT", "big", "qko", "vtok", "mrg", "att"))
        h_hi, h_lo = parts["mrg"], parts["qko"]
        act_hi = [parts["big"][:, 512 * i:512 * i + 512] for i in range(FC // 2)]
        act_lo = [parts["att"][:, 2560 + 512 * i:][:, 0:512] for i in range(3)]
        act_lo += [parts["vtok"][:, 512 * i:512 * i + 512] for i in range(2)]
        act_lo += [parts["qko"][:, 2048 + 512 * i:][:, 0:512] for i in range(2)]
        act_lo += [parts["hT"][:, 512 * i:512 * i + 512] for i in range(4)]
        const = sb("const", CWID)
        par = sb("par", PW)
        xT = sb("xT", DC * T)
        sq = sb("sq", DC * T)
        pad = sb("pad", 4 * (T + CW - 1))
        rs2 = [sb(f"rs{i}", 512) for i in range(2)]
        st = sb("st", 128)
        w_f = sb("w_f", DC * 4)
        count_i = sb("count_i", 1, I32)
        bank = [ctx.enter_context(nc.psum_tensor(f"bank{i}", [P, 512], F32)) for i in range(8)]

        FORGET = 4096

        def item(at):
            return att[:, at:at + 512] if at < 4096 else sq[:, at - 4096:at - 4096 + 512]

        def C(name, parts=slice(0, P)):
            a, b = CAT[name]
            return const[parts, a:b]

        def W(name, parts=slice(0, P)):
            a, b = PAT[name]
            return par[parts, a:b]

        def col(name, i, parts=slice(0, P)):
            a, _ = PAT[name]
            return par[parts, a + i:a + i + 1]

        def ch(t, i, n=1, w=T):
            v = t[:, i * w:(i + n) * w]
            return v if n == 1 else v.rearrange("p (c t) -> p c t", c=n)

        def flat(t, a, n):
            return t[:, a:a + n]

        full = [sem(f"bank_full{i}") for i in range(8)]
        empty = [sem(f"bank_empty{i}") for i in range(8)]
        landed = [sem(f"weights_landed{i}") for i in range(RING)]
        used = [sem(f"weights_used{i}") for i in range(RING)]
        landed_post = [sem(f"weights_landed_post{i}") for i in range(RING)]
        used_post = [sem(f"weights_used_post{i}") for i in range(RING)]
        raw_landed = {stage: [sem(f"raw_landed_{stage}{i}") for i in range(2)] for stage in ("in", "ff")}
        names = """x_hi x_lo up_tap in_hi in_lo in_lo_first h1_hi h1_lo ff_hi ff_lo_pool ff_lo_dve pair_used h_hi h_lo up_val act_hi act_lo const_in par_in x_in pos_in wf_in mem_in out_done dve_step act_step zeroed squares normed lam_in
                   lam_exp qk_ready s_max s_exp a_ready conved conv_dev conv_z conv_sig conv_out attn_out merged
                   logits pair_gap g_exp e_exp member rounds picked pick_step hid_step swt_full rows_full swt rows gate_sig
                   hidden hid_full hidT y_out comb_full added experts_done pos_f ang trig rope rows_zero f_abs f_exp
                   c_rows z_pool y_mix pads_zero up_conv up_sig""".split()
        S = {n: sem(n) for n in names}
        count = {}

        def signal(ins, name, by=1):
            ins.then_inc(S[name], by)
            count[name] = count.get(name, 0) + by
            return count[name]

        def done(eng, ins, name):
            eng.wait_ge(S[name], signal(ins, name))

        def begin(pe, use):
            b, n = PLACE[use]
            if n > 1:
                pe.wait_ge(empty[b], n - 1)
            return bank[b]

        def filled(ins, use):
            ins.then_inc(full[PLACE[use][0]], 1)

        def arrive(eng, use):
            b, n = PLACE[use]
            eng.wait_ge(full[b], n)
            return bank[b]

        def emptied(ins, use):
            ins.then_inc(empty[PLACE[use][0]], 1)

        def copied(eng, use):
            b, n = PLACE[use]
            eng.wait_ge(empty[b], n)

        w_in = A["w_in"][0].rearrange("(k p) n -> p k n", p=P)
        w_co = A["w_conv_out"][0].rearrange("(k p) n -> p k n", p=P)
        w_ao = A["w_attn_out"][0].rearrange("(k p) n -> p k n", p=P)
        w_o = A["w_out"][0].rearrange("(k p) n -> p k n", p=P)
        w_in_units = [[w_in[:, :, 512 * i:512 * i + 512]] for i in range(9)]
        pre = [w_co, w_ao]
        pre += [w_o[:, :, 512 * i:512 * i + 512] for i in range(2)]
        w_in2 = A["w_in_2"][0].rearrange("(k p) n -> p k n", p=P)
        w_o2 = A["w_out_2"][0].rearrange("(k p) n -> p k n", p=P)
        w_xkv = A["w_xkv_2"][0].rearrange("(k p) n -> p k n", p=P)
        pre += [w_xkv[:, :, 512 * i:512 * i + 512] for i in range(2)]
        assert len(pre) == PRE_UNITS
        w_xq = A["w_xq_2"][0].rearrange("(k p) n -> p k n", p=P)
        w_xo = A["w_xo_2"][0].rearrange("(k p) n -> p k n", p=P)
        w_up = A["w_up_2"][0].rearrange("(k p) (a n) -> p k a n", p=P, a=2)
        w_dn = A["w_down_2"][0].rearrange("(k p) n -> p k n", p=P)

        def halves(w, i):
            return [w[:, :, 512 * i:512 * i + 512]]

        post = [halves(w_xkv, 2)] + [halves(w_in2, i) for i in (1, 2, 3)] + [halves(w_xkv, 3)]
        post += [[w_in2[:, :, 2048:2304], w_in2[:, :, 2308:2564]], halves(w_in2, 0)]
        ffn = [halves(w, i) for w in (w_o2, w_xq, w_xo) for i in range(2)]
        FIRST_UP = len(ffn)
        ffn += [[w_up[:, :, a, 256 * i:256 * i + 256] for a in range(2)] for i in range(11)]
        FIRST_DN = len(ffn)
        ffn += [[w_dn[:, 4 * i:min(4 * i + 4, FC), :]] for i in range(6)]

        slot_raw, slot_even, slot_odd = ((PRE_UNITS + j) % RING for j in (1, 3, 5))
        split = {"in": w_in_units, "ff": ffn}
        raws = {"in": [ring[1], ring[0]], "ff": [ring[(slot_raw + i) % RING] for i in range(2)]}
        pairs = {"in": [[ring_r[4], ring_r[5]], [ring_r[2], ring_r[3]]],
                 "ff": [[ring_r[(s + i) % RING] for i in range(2)] for s in (slot_even, slot_odd)]}
        words = {n: [UW if len(u) == 2 else u[0].shape[1] * u[0].shape[2] for u in us] for n, us in split.items()}
        raw_count = {}
        for n, us in split.items():
            n_raw = [0, 0]
            raw_count[n] = []
            for u, halves_ in enumerate(us):
                n_raw[u % 2] += 16 * len(halves_)
                raw_count[n].append(n_raw[u % 2])
        IN_LAST = [("ca", 3), ("cg", 3), ("q", 3), ("k", 3), ("v", 1)] + [("gt", 4 * i + 3) for i in range(4)]
        h1_hi = [parts["qko"][:, 2048 + T * k:][:, 0:T] for k in range(4)]
        h1_hi += [parts["mrg"][:, 1024 + T * k:][:, 0:T] for k in range(4)]
        h1_lo = parts["hT"]

        def load_raw(sp, stage, u):
            src, sem_ = split[stage][u], raw_landed[stage][u % 2]
            if len(src) == 2:
                both = raws[stage][u % 2][:, :].rearrange("p (k a n) -> p k a n", k=8, a=2)
                for a in range(2):
                    sp.dma_start(both[:, :, a], src[a]).then_inc(sem_, 16)
            else:
                dst = raws[stage][u % 2][:, 0:words[stage][u]].rearrange("p (k n) -> p k n", k=src[0].shape[1])
                sp.dma_start(dst, src[0]).then_inc(sem_, 16)

        def round_unit(act, stage, u):
            act.wait_ge(raw_landed[stage][u % 2], raw_count[stage][u])
            h = words[stage][u] // 2
            for i in range(2):
                part = slice(i * h, i * h + h)
                signal(act.activation(pairs[stage][u % 2][0][:, part], raws[stage][u % 2][:, part], ACT.Copy), stage + "_hi")

        def rest_of_unit(eng, stage, u, i, name):
            h = words[stage][u] // 2
            hi, lo = pairs[stage][u % 2]
            part = slice(i * h, i * h + h)
            eng.wait_ge(S[stage + "_hi"], 2 * u + i + 1)
            signal(eng.tensor_tensor(lo[:, part], raws[stage][u % 2][:, part], hi[:, part].bitcast(F32), ALU.subtract), name)

        FF_FREE = [("vx", 3), ("pa", 3)] + [(k, m) for k in ("w2", "qx", "xo") for m in (3, 7)] + [("ug", i) for i in range(11)]
        parts_landed = {}
        seen = [0] * RING
        for j, u in enumerate(post):
            s = (PRE_UNITS + j) % RING
            seen[s] += 16 * len(u)
            parts_landed[j] = seen[s]

        def pre_unit(pe, i):
            pe.wait_ge(landed[i % RING], 16 * (i // RING + 1))
            return ring[i % RING]

        def post_unit(pe, j):
            s = (PRE_UNITS + j) % RING
            pe.wait_ge(landed_post[s], parts_landed[j])
            return ring[s]

        def u512(slot):
            return slot[:, :].rearrange("p (k n) -> p k n", k=8)

        def u1024(slot):
            return slot[:, :].rearrange("p (k n) -> p k n", k=4)

        o = 0

        def carve(n):
            nonlocal o
            o += n
            return big[:, o - n:o]

        xeT = carve(DC * P).rearrange("p (k s) -> p k s", k=DC)
        sig = carve(512)
        hid = carve(512)
        hidT = carve(512).rearrange("p (k s) -> p k s", k=4)
        y_e = carve(D)
        swT = carve(T)
        pick = carve(TT * P).rearrange("p (t j s) -> p t j s", t=TT, j=QUAD)
        wpick = carve(TT * P).rearrange("p (t j s) -> p t j s", t=TT, j=QUAD)
        slot_of = carve(TT * ROUNDS * NE).rearrange("p (t r) -> p t r", t=TT)
        weight_of = carve(TT * ROUNDS * NE).rearrange("p (t r) -> p t r", t=TT)
        h2tok = ch(att, 0, TT, D)
        NORMS = {n: 8 * i for i, n in enumerate(("n1", "nmem", "n2", "nmix", "nxa", "nffn", "nfin"))}
        SQUARES = {n: 2 * i for i, n in enumerate(("n1", "qn", "kn", "var", "on", "nmem", "n2", "nmix", "nxa", "nffn", "nfin"))}
        ROOTS = [(("n1", 0), T, D)] + [((k, i), 512, 64) for k in ("qn", "kn") for i in range(2)]
        ROOTS += [(("var", 0), T, 512)] + [(("on", i), 512, P) for i in range(2)]
        ROOTS += [((k, 0), T, D) for k in ("nmem", "n2", "nmix", "nxa", "nffn", "nfin")]
        TURN = {use: i % 2 for i, (use, _, _) in enumerate(ROOTS)}


        ro = 2048

        def small(*shape):
            nonlocal ro
            n = int(np.prod(shape))
            v = qko[:, ro:ro + n]
            ro += n
            if len(shape) == 1:
                return v
            names = "abc"[:len(shape)]
            return v.rearrange(f"p ({' '.join(names)}) -> p {' '.join(names)}", **dict(zip(names, shape)))

        member = small(TT, NG, EG)
        e_all = small(TT, NG, EG)
        logit = small(TT, 36)
        place_of = small(TT, NE)
        g_hot, g_tmp = small(TT, NG), small(TT, NG)
        g_gap = small(TT * NG)
        g_gap3 = g_gap.rearrange("p (t g) -> p t g", t=TT)
        e_val, e_tmp, hot1, hot2 = (small(TT, EG) for _ in range(4))
        g_max, g_sum, e_max1, e_max2, e_gap, w_1, w_2, tie = (small(TT) for _ in range(8))
        assert ro <= 3072
        pool_x = qko[:, 0:544].rearrange("p (c t) -> p c t", c=2)
        pool_s = [qko[:, 544 * i:544 * i + 544].rearrange("p (c t) -> p c t", c=2) for i in (1, 2)]
        z_pool = qko[:, 1632:2144]
        conv_x = pad[:, 512:1028].rearrange("p (c t) -> p c t", c=2)
        f_z, f_abs, f_e = (big[0:4, 4612 + T * i:4612 + T * i + T] for i in range(3))
        c_rows = qko[:, 2144:2144 + 2 * T]
        c_row, neg_c = (c_rows[:, T * i:T * i + T] for i in range(2))
        f_zero = qko[0:4, 2144 + 2 * T:2144 + 3 * T]
        qc_head = [ch(big, i) for i in (10, 11, 16, 17)]
        mean_row = big[:, 20 * T:21 * T]
        st_pos = rs2[0][:, 0:T]
        pos_i = pad[0:1, 0:T].bitcast(I32)
        up_x = pad[:, 0:4 * (T + 2)].rearrange("p (c t) -> p c t", c=4)
        up_ys, up_s = [att[:, 1024 * i:1024 * i + 1024] for i in range(2)], att[:, 2048:2560]
        up_vals = [sq[:, 512 * i:512 * i + 512] for i in range(2)]

        block = ctx.enter_context(nc.Block())

        @block.sync
        def _(sp):
            sp.dma_start(const[:, :], A["const"]).then_inc(S["const_in"], 16)
            sp.dma_start(par[:, :], A["par"]).then_inc(S["par_in"], 16)
            for u in range(9):
                if u >= 2:
                    sp.wait_ge(S["in_lo"], 2 * u - 3)
                if u == 2:
                    sp.wait_ge(S["in_lo_first"], 1)
                load_raw(sp, "in", u)
            for i, src in enumerate(pre):
                if i < 2:
                    sp.wait_ge(S["in_lo"], 15 + 2 * i)
                else:
                    arrive(sp, ("gt", 11 if i < 4 else 15))
                dst = ring[i % RING][:, :].rearrange("p (k n) -> p k n", k=src.shape[1])
                sp.dma_start(dst, src).then_inc(landed[i % RING], 16)

            w_g = A["w_gate_e"][0].rearrange("(q j) (u p c) n -> q u p j (c n)", j=QUAD, c=2, p=P)
            w_u = A["w_up_e"][0].rearrange("(q j) (u p c) n -> q u p j (c n)", j=QUAD, c=2, p=P)
            w_d = A["w_down_e"][0].rearrange("(q j) (u p) n -> q u p j n", j=QUAD, p=P)

            def step(q, n):
                for u in range(EUNITS):
                    i = PRE_UNITS + u
                    s = i % RING
                    sp.wait_ge(used[s], n * (EUNITS // RING) + i // RING)
                    w = (w_g, w_u, w_d)[u // 4]
                    sp.dma_start(ring[s][:, :].rearrange("p (j n) -> p j n", j=QUAD),
                                 w[bass.ds(q, 1), u % 4].rearrange("q p j n -> p (q j) n")).then_inc(landed[s], 16)

            with sp.Fori(0, QUADS) as q:
                step(q, q)
            sp.wait_ge(S["rounds"], 1)
            steps = sp.value_load(count_i[0:1, 0:1], min_val=QUADS, max_val=QUADS * ROUNDS)
            with sp.If(steps > QUADS):
                with sp.Fori(QUADS, steps) as n:
                    step(n % QUADS, n)
            with sp.Else():
                pass
            for j, parts in enumerate(post):
                i = PRE_UNITS + j
                s = i % RING
                if j < RING:
                    sp.wait_ge(used[s], steps * (EUNITS // RING) + i // RING)
                else:
                    sp.wait_ge(used_post[s], j // RING)
                if len(parts) == 2:
                    both = ring[s][:, :].rearrange("p (k a n) -> p k a n", k=8, a=2)
                    for a in range(2):
                        sp.dma_start(both[:, :, a], parts[a]).then_inc(landed_post[s], 16)
                else:
                    kn, n = parts[0].shape[1], parts[0].shape[2]
                    dst = ring[s][:, 0:kn * n].rearrange("p (k n) -> p k n", k=kn)
                    sp.dma_start(dst, parts[0]).then_inc(landed_post[s], 16)
            for u in range(len(ffn)):
                if u < 2:
                    arrive(sp, (("qb", 1), ("vb", 1))[u])
                else:
                    for half in ("pool", "dve"):
                        sp.wait_ge(S["ff_lo_" + half], u - 1)
                load_raw(sp, "ff", u)
            for i in range(4):
                copied(sp, ("out", i))
            sp.dma_start(out[0].rearrange("(t p) d -> p t d", p=P), ch(att, 0, TT, D)).then_inc(S["out_done"], 16)
            sp.wait_ge(S["out_done"], 16)

        @block.gpsimd
        def _(pool):
            pool.memset(pad[:, :], 0.0).then_inc(S["zeroed"], 1)

            for u in range(9):
                for i in range(2 if u else 1):
                    rest_of_unit(pool, "in", u, i, "in_lo")
            for u in range(len(ffn)):
                rest_of_unit(pool, "ff", u, 0, "ff_lo_pool")

        @block.tensor
        def _(pe):
            ident, ones = C("ident"), C("ones")
            freed = []

            def tell(mm):
                if freed:
                    mm.then_inc(freed.pop(0), 1)

            def norm_sum(use, src, n=8):
                b = begin(pe, use)
                for c in range(n):
                    if c % (n // 2) == 0:
                        pe.wait_ge(S["squares"], SQUARES[use[0]] + c // (n // 2) + 1)
                    mm = pe.matmul(b[:, 0:T], ones, src[:, c * T:c * T + T], start=(c == 0), stop=(c == n - 1))
                    if c < n - 1:
                        tell(mm)
                filled(mm, use)

            def linear(use, w, m, src, kn=8, at=0, norm=None, last=True):
                b = begin(pe, use) if at == 0 else bank[PLACE[use][0]]
                for k in range(kn):
                    if norm is not None:
                        pe.wait_ge(S["normed"], NORMS[norm] + k + 1)
                    mm = pe.matmul(b[:, at:at + T], w[:, k, P * m:P * m + P], src[:, k * T:k * T + T],
                                   start=(k == 0), stop=(k == kn - 1))
                    if k < kn - 1:
                        tell(mm)
                if last:
                    filled(mm, use)

            def values(use, w, t, n0, n, src):
                b = begin(pe, use)
                for k in range(8):
                    mm = pe.matmul(b[:, 0:n], src[:, k * T + P * t:k * T + P * t + P], w[:, k, n0:n0 + n],
                                   start=(k == 0), stop=(k == 7))
                    if k < 7:
                        tell(mm)
                filled(mm, use)

            def turn(use, parts):
                b = begin(pe, use)
                for at, src in parts:
                    mm = pe.transpose(b[:, at:at + P], src, ident)
                filled(mm, use)

            def scores(use, parts):
                b = begin(pe, use)
                for at, n, lhsT, rhs, first, last in parts:
                    mm = pe.matmul(b[:, at:at + n], lhsT, rhs, start=first, stop=last)
                filled(mm, use)

            pe.wait_ge(S["const_in"], 16)
            pe.wait_ge(S["x_in"], 16)
            xtok = ch(att, 0, TT, D)
            for i in range(4):
                turn(("xT", i), [(c * T + t * P, xtok[:, t, (2 * i + c) * P:(2 * i + c + 1) * P])
                                 for c in range(2) for t in range(TT)])
            pe.wait_ge(S["lam_in"], 1)
            b = begin(pe, ("lam", 0))
            filled(pe.matmul(b[:, 0:2], ones, st[:, 100:102], start=True, stop=True), ("lam", 0))
            norm_sum(("n1", 0), sq)
            IN = [[t[:, :].rearrange("p (k n) -> p k n", k=8) for t in pair] for pair in pairs["in"]]

            def project(u, use, first):
                w_hi, w_lo = IN[u % 2]
                for m in range(4):
                    b = begin(pe, (use, first + m))
                    for which, w in enumerate((w_hi, w_lo, w_hi)):
                        for k in range(8):
                            if m == 0 and which == 0 and k % 4 == 0:
                                pe.wait_ge(S["in_hi"], 2 * u + k // 4 + 1)
                            if m == 0 and which == 1 and k % 4 == 0:
                                if u:
                                    pe.wait_ge(S["in_lo"], 2 * u + k // 4)
                                else:
                                    pe.wait_ge(S[("in_lo", "in_lo_first")[k // 4]], 1)
                            if (u, m) == (0, 0) and which != 1 and k % 4 == 0:
                                pe.wait_ge(S["h1_hi" if which == 0 else "h1_lo"], k // 4 + 1)
                            x = h1_hi[k] if which < 2 else h1_lo[:, k * T:k * T + T]
                            mm = pe.matmul(b[:, 0:T], w[:, k, P * m:P * m + P], x,
                                           start=(which == 0 and k == 0), stop=(which == 2 and k == 7))
                    filled(mm, (use, first + m))

            for u, use in enumerate(("ca", "cg", "q", "k")):
                project(u, use, 0)
            w_hi, w_lo = IN[0]
            pe.wait_ge(S["in_hi"], 10)
            pe.wait_ge(S["in_lo"], 9)
            for t in range(TT):
                b = begin(pe, ("v", t))
                for which, w in enumerate((w_hi, w_hi, w_lo)):
                    for k in range(8):
                        x = h1_lo[:, k * T + P * t:k * T + P * t + P] if which == 1 else h1_hi[k][:, P * t:P * t + P]
                        mm = pe.matmul(b[:, :], x, w[:, k], start=(which == 0 and k == 0), stop=(which == 2 and k == 7))
                filled(mm, ("v", t))

            def gates(u):
                project(5 + u, "gt", 4 * u)

            for use in ("qn", "kn"):
                for i in range(2):
                    b = begin(pe, (use, i))
                    pe.wait_ge(S["squares"], SQUARES[use] + i + 1)
                    src = sq[:, 512 * i + (1024 if use == "kn" else 0):][:, 0:512]
                    filled(pe.matmul(b[:, :], C("blk64"), src, start=True, stop=True), (use, i))

            def block1_scores(h):
                pe.wait_ge(S["qk_ready"], 4)
                for c in range(2):
                    scores(("s1", 2 * h + c),
                           [(t * T, T, qko[64 * c:64 * c + 64, h * T + t * P:h * T + t * P + P],
                             qko[64 * c:64 * c + 64, (4 + h) * T:(5 + h) * T], True, True) for t in range(TT)])

            gates(0)
            gates(1)
            block1_scores(0)
            block1_scores(1)
            b = begin(pe, ("mu", 0))
            for c in range(4):
                pe.wait_ge(S["conved"], c + 1)
                mm = pe.matmul(b[:, 0:T], ones, big[:, (16 + c) * T:(17 + c) * T], start=(c == 0), stop=(c == 3))
            filled(mm, ("mu", 0))
            block1_scores(2)
            block1_scores(3)
            gates(2)
            norm_sum(("var", 0), sq[:, 1024:2048], 4)
            gates(3)
            w = u1024(pre_unit(pe, 0))
            pe.wait_ge(S["conv_out"], 1)
            for m in range(8):
                linear(("co", m), w, m, big[:, 16 * T:20 * T], 4)
            freed.append(used[0])
            for h in range(4):
                pe.wait_ge(S["a_ready"], 2 * h + 2)
                turn(("aT1", h), [(kt * T + t * P, att[:, 1024 * h + T * t + kt * P:][:, 0:P])
                                  for t in range(TT) for kt in range(2)])
            for t in range(TT):
                copied(pe, ("v", t))
            for h in range(4):
                copied(pe, ("aT1", h))
                scores(("o1", h), [(0, T, vtok[:, 512 * kt + P * h:][:, 0:P], sq[:, 512 * h + T * kt:][:, 0:T],
                                    kt == 0, kt == 1) for kt in range(2)])
            for i in range(2):
                b = begin(pe, ("on", i))
                pe.wait_ge(S["squares"], SQUARES["on"] + i + 1)
                filled(pe.matmul(b[:, :], ones, sq[:, 512 * i:512 * i + 512], start=True, stop=True), ("on", i))
            pe.wait_ge(S["mem_in"], 16)
            memtok = att[:, 2048:4096].rearrange("p (t d) -> p t d", t=TT)
            for i in range(4):
                turn(("mT", i), [(c * T + t * P, memtok[:, t, (2 * i + c) * P:(2 * i + c + 1) * P])
                                 for c in range(2) for t in range(TT)])
            w = u1024(pre_unit(pe, 1))
            pe.wait_ge(S["attn_out"], 2)
            for m in range(8):
                linear(("ao", m), w, m, qko[:, 8 * T:12 * T], 4)
            freed.append(used[1])
            for u in range(2):
                w = u512(pre_unit(pe, 2 + u))
                if u == 0:
                    pe.wait_ge(S["merged"], 8)
                for m in range(4):
                    linear(("wo", 4 * u + m), w, m, mrg)
                freed.append(used[2 + u])
                if u == 0:
                    norm_sum(("nmem", 0), big)

            def mem_keys(ms):
                for m in ms:
                    if m % 4 == 0:
                        pre_unit(pe, 4 + m // 4)
                    linear(("kx", m), u512(ring[4 + m // 4]), m % 4, qko, norm="nmem" if m == 0 else None)
                    if m % 4 == 3:
                        freed.append(used[4 + m // 4])

            mem_keys((0, 1))
            norm_sum(("n2", 0), sq)
            mem_keys((2, 3))
            pe.wait_ge(S["normed"], NORMS["n2"] + 8)
            wr = W("w_r").rearrange("p (k n) -> p k n", k=DC)
            for t in range(TT):
                b = begin(pe, ("rt", t))
                for k in range(DC):
                    pe.matmul(b[:, 0:36], hT[:, k * T + P * t:k * T + P * t + P], wr[:, k], start=(k == 0), stop=False)
                filled(pe.matmul(b[:, 0:36], ones, W("b_r"), start=False, stop=True), ("rt", t))

            for t in range(TT):
                for half in range(2):
                    turn(("h2t", 2 * t + half), [(c * P, hT[:, (4 * half + c) * T + t * P:][:, 0:P]) for c in range(4)])
            mem_keys((4, 5, 6, 7))
            pe.wait_ge(S["member"], 1)
            mem = [member[:, t].rearrange("p g j -> p (g j)") for t in range(TT)]
            for use, terms in ((("pos", 0), (("before", 0),)), (("pos", 1), (("ones", 0), ("before", 1))),
                               (("cnt", 0), (("ones", 0), ("ones", 1)))):
                scores(use, [(0, NE, C(a), mem[t], i == 0, i == len(terms) - 1) for i, (a, t) in enumerate(terms)])
            for m in range(4, 8):
                copied(pe, ("kx", m))
            pe.wait_ge(full[PLACE[("kx", 7)][0]], PLACE[("kx", 7)][1])
            assert len(freed) == 1
            pe.sem_inc(freed.pop(), 1)
            for i in range(4):
                copied(pe, ("h2t", i))
            for use in (("rt", 0), ("rt", 1), ("pos", 0), ("pos", 1), ("cnt", 0), ("n2", 0)):
                copied(pe, use)
            pe.wait_ge(S["rounds"], 1)
            steps = pe.value_load(count_i[0:1, 0:1], min_val=QUADS, max_val=QUADS * ROUNDS)
            pe.sem_inc(S["rows_full"], 1)
            with pe.Fori(0, steps) as n:
                pe.wait_ge(S["picked"], n * 2 + 2)
                pe.wait_ge(S["added"], n * 4 + 1)
                for t in range(TT):
                    mm = pe.transpose(bank[4][:, t * P:t * P + P], wpick[:, t].rearrange("p j s -> p (j s)"), ident)
                mm.then_inc(S["swt_full"], 1)
                for k in range(DC):
                    for t in range(TT):
                        rows = h2tok[:, t, 256 * (k // 2) + k % 2:256 * (k // 2) + k % 2 + 255:2]
                        mm = pe.matmul(bank[5 + k // 4][:, P * (k % 4):P * (k % 4) + P], rows,
                                       pick[:, t].rearrange("p j s -> p (j s)"), start=(t == 0), stop=(t == TT - 1))
                    if k % 4 == 3:
                        mm.then_inc(S["rows_full"], 1)

                def unit(u):
                    i = PRE_UNITS + u
                    pe.wait_ge(landed[i % RING], n * (16 * EUNITS // RING) + 16 * (i // RING + 1))
                    return ring[i % RING], used[i % RING]

                pe.wait_ge(S["rows"], n * 2 + 2)
                pe.wait_ge(S["hidden"], n + 1)
                for part in range(2):
                    for u in range(4):
                        slot, free = unit(4 * part + u)
                        w = slot[:, :].rearrange("p (j c n) -> p j c n", j=QUAD, c=2)
                        for c in range(2):
                            for j in range(QUAD):
                                mm = pe.matmul(bank[part][CAP * j:CAP * j + CAP, :],
                                               xeT[:, 2 * u + c, CAP * j:CAP * j + CAP], w[:, j, c],
                                               start=(u == 0 and c == 0), stop=(u == 3 and c == 1))
                        mm.then_inc(free, 1)
                pe.wait_ge(S["hidden"], n + 2)
                for k in range(4):
                    mm = pe.transpose(bank[7][:, P * k:P * k + P], hid[:, P * k:P * k + P], ident)
                mm.then_inc(S["hid_full"], 1)
                pe.wait_ge(S["hidT"], n + 1)
                pe.wait_ge(S["y_out"], n * 2 + 1)
                for u in range(4):
                    slot, free = unit(8 + u)
                    w = slot[:, :].rearrange("p (j n) -> p j n", j=QUAD)
                    for half in range(2):
                        for j in range(QUAD):
                            mm = pe.matmul(bank[2 + half][CAP * j:CAP * j + CAP, :],
                                           hidT[:, u, CAP * j:CAP * j + CAP], w[:, j, 512 * half:512 * half + 512],
                                           start=(u == 0), stop=(u == 3))
                    mm.then_inc(free, 1)
                pe.wait_ge(S["swt"], n + 1)
                pe.wait_ge(S["y_out"], n * 2 + 3)
                for m in range(DC):
                    mm = pe.matmul(bank[4 + m // 2][:, T * (m % 2):T * (m % 2) + T], y_e[:, P * m:P * m + P], swT,
                                   start=True, stop=True)
                    if m % 2:
                        mm.then_inc(S["comb_full"], 1)

            pe.wait_ge(S["experts_done"], 1)
            pe.wait_ge(S["pos_f"], 1)
            b = begin(pe, ("posb", 0))
            filled(pe.matmul(b[:, 0:T], C("ones", slice(0, 1)), st_pos[0:1, :], start=True, stop=True), ("posb", 0))
            norm_sum(("nmix", 0), sq)

            def post_free(j):
                freed.append(used_post[(PRE_UNITS + j) % RING])

            def mem_values(j, u):
                w = u512(post_unit(pe, j))
                for t in range(TT):
                    values(("vx", 2 * u + t), w, t, 0, 512, qko)
                post_free(j)

            mem_values(0, 0)
            w = u512(post_unit(pe, 1))
            for m, use in enumerate((("pa", 4), ("pa", 5), ("qb", 0), ("qb", 1))):
                linear(use, w, m, hT, norm="nmix" if m == 0 else None)
            post_free(1)
            w = u512(post_unit(pe, 2))
            for m in range(2):
                linear(("kb", m), w, m, hT)
            for t in range(TT):
                values(("vb", t), w, t, 256, 256, hT)
            post_free(2)
            for use, last, at in (("rq", "qb", 6), ("rk", "kb", 8)):
                for m in range(2):
                    copied(pe, (last, m))
                scores((use, 0), [(0, 512, C("rot"), big[:, at * T:(at + 2) * T], True, True)])
            w = u512(post_unit(pe, 3))
            for m in range(4):
                linear((("qc", "kc")[m // 2], m % 2), w, m, hT)
            post_free(3)
            b = begin(pe, ("f", 0))
            pe.wait_ge(S["wf_in"], 16)
            for k in range(8):
                mm = pe.matmul(b[0:4, 0:T], w_f[:, 4 * k:4 * k + 4], hT[:, k * T:k * T + T], start=(k == 0), stop=(k == 7))
                if k < 7:
                    tell(mm)
            filled(mm, ("f", 0))
            pe.wait_ge(S["rope"], 2)
            for h in range(4):
                r, m = slice(64 * (h % 2), 64 * (h % 2) + 64), h // 2
                scores(("sb", h), [(t * T, T, big[r, (6 + m) * T + t * P:][:, 0:P], big[r, (8 + m) * T:(9 + m) * T], True, True)
                                   for t in range(TT)])
            mem_values(4, 1)
            for use in ("qc", "kc"):
                for m in range(2):
                    copied(pe, (use, m))
            pe.wait_ge(S["c_rows"], 2)
            sel = C("sel").rearrange("p (h n) -> p h n", h=4)
            for h in range(4):
                terms = []
                for t in range(TT):
                    terms += [(t * T, T, qc_head[h][:, t * P:t * P + P], big[:, (12 + h // 2) * T:(13 + h // 2) * T], True, False),
                              (t * T, T, sel[:, h], neg_c, False, False)]
                    terms += [(t * T + P * kt, P, c_row[:, t * P:t * P + P], sel[:, h], False, kt == 1) for kt in range(2)]
                scores(("sc", h), terms)
            w = post_unit(pe, 5)[:, :].rearrange("p (k a n) -> p k a n", k=8, a=2)
            for t in range(TT):
                values(("vc", t), w[:, :, 0], t, 0, 256, hT)
            for m in range(2):
                linear(("pd", m), w[:, :, 1], m, hT)
            post_free(5)
            w = u512(post_unit(pe, 6))
            for m in range(4):
                linear(("pa", m), w, m, hT)
            post_free(6)

            def small_attention(name, base, first_item):
                for h in range(4):
                    pe.wait_ge(S["a_ready"], first_item + h + 1)
                    turn(("aT" + name, h), [(kt * T + t * P, item(base + 512 * h)[:, T * t + kt * P:][:, 0:P])
                                            for t in range(TT) for kt in range(2)])

            def heads_out(name, base, v0, uses_v):
                for t in range(TT):
                    copied(pe, (uses_v, t))
                for h2 in range(2):
                    b = begin(pe, ("o" + name, h2))
                    for c in range(2):
                        h = 2 * h2 + c
                        copied(pe, ("aT" + name, h))
                        for kt in range(2):
                            mm = pe.matmul(b[64 * c:64 * c + 64, 0:T], vtok[:, 512 * kt + v0 + 64 * h:][:, 0:64],
                                           item(base + 512 * h)[:, T * kt:][:, 0:T], start=(kt == 0), stop=(kt == 1))
                    filled(mm, ("o" + name, h2))

            small_attention("b", 0, 8)
            heads_out("b", 0, 0, "vb")
            pe.wait_ge(S["z_pool"], 1)
            wp = W("w_pool")
            scores(("pl", 0), [(c * T, T, wp[:, c * P:c * P + P], z_pool[:, c * T:c * T + T], True, True) for c in range(2)])
            small_attention("c", FORGET, 12)
            heads_out("c", FORGET, 256, "vc")
            def split_unit(u, form, **dims):
                pe.wait_ge(S["ff_hi"], 2 * u + 2)
                return [t[:, 0:words["ff"][u]].rearrange(form, **dims) for t in pairs["ff"][u % 2]]

            def split_linear(use, u0, hi, lo, stage, after=None):
                for u in (u0, u0 + 1):
                    w_hi, w_lo = split_unit(u, "p (k n) -> p k n", k=8)
                    for m in range(4):
                        out_use = (use, 4 * (u - u0) + m)
                        b = begin(pe, out_use)
                        for which, (w, x) in enumerate(((w_hi, hi), (w_lo, hi), (w_hi, lo))):
                            if m == 0 and which == 1:
                                for half in ("pool", "dve"):
                                    pe.wait_ge(S["ff_lo_" + half], u + 1)
                            for k in range(8):
                                if (u, m) == (u0, 0) and which != 1 and k % 4 == 0:
                                    pe.wait_ge(S["x_hi" if which == 0 else "x_lo"], 2 * stage + k // 4 + 1)
                                mm = pe.matmul(b[:, 0:T], w[:, k, P * m:P * m + P], x[:, k * T:k * T + T],
                                               start=(which == 0 and k == 0), stop=(which == 2 and k == 7))
                                if not (which == 2 and k == 7):
                                    tell(mm)
                        filled(mm, out_use)
                    if after:
                        after(u - u0)

            split_linear("w2", 0, parts["big"][:, 0:2048], parts["hT"], 0)
            norm_sum(("nxa", 0), sq)

            def cross_scores(u):
                for h in (2 * u, 2 * u + 1):
                    for e in range(2):
                        copied(pe, ("kx", 2 * h + e))
                        copied(pe, ("qx", 2 * h + e))
                    scores(("sx", h), [(t * T, T, qko[:, (2 * h + e) * T + t * P:][:, 0:P],
                                        att[:, (8 + 2 * h + e) * T:(9 + 2 * h + e) * T], e == 0, e == 1)
                                       for t in range(TT) for e in range(2)])

            split_linear("qx", 2, parts["big"][:, 2048:4096], parts["hT"], 1, cross_scores)
            small_attention("x", 0, 16)
            for i in range(4):
                copied(pe, ("vx", i))
            for h in range(4):
                copied(pe, ("aTx", h))
                scores(("ox", h), [(e * T, T, mrg[:, 1024 * kt + 256 * h + P * e:][:, 0:P], sq[:, 512 * h + T * kt:][:, 0:T],
                                    kt == 0, kt == 1) for e in range(2) for kt in range(2)])
            split_linear("xo", 4, parts["hT"], parts["big"][:, 0:2048], 2)
            norm_sum(("nffn", 0), sq)
            for i in range(11):
                w_hi, w_lo = split_unit(FIRST_UP + i, "p (k a n) -> p k a n", k=8, a=2)
                for a, use in enumerate(("ua", "ug")):
                    b = begin(pe, (use, i))
                    for m in range(2):
                        for which, (w, x) in enumerate(((w_hi, h_hi), (w_lo, h_hi), (w_hi, h_lo))):
                            if (a, m, which) == (0, 0, 1):
                                for half in ("pool", "dve"):
                                    pe.wait_ge(S["ff_lo_" + half], FIRST_UP + i + 1)
                            for k in range(8):
                                if (i, a, m) == (0, 0, 0) and which != 1 and k % 4 == 0:
                                    pe.wait_ge(S["h_hi" if which == 0 else "h_lo"], k // 4 + 1)
                                mm = pe.matmul(b[:, T * m:T * m + T], w[:, k, a, P * m:P * m + P], x[:, k * T:k * T + T],
                                               start=(which == 0 and k == 0), stop=(which == 2 and k == 7))
                                if not (m == 1 and which == 2 and k == 7):
                                    tell(mm)
                    filled(mm, (use, i))
            for i in range(6):
                u = FIRST_DN + i
                w_hi, w_lo = split_unit(u, "p (k n) -> p k n", k=words["ff"][u] // D)
                for half in ("pool", "dve"):
                    pe.wait_ge(S["ff_lo_" + half], u + 1)
                ks = range(4 * i, min(4 * i + 4, FC))
                for m in range(8):
                    if i == 0:
                        begin(pe, ("dn", m))
                    for k in ks:
                        if m == 0:
                            pe.wait_ge(S["act_lo"], k // 2 + 1)
                        at = (k % 2) * T
                        for which, (w, x) in enumerate(((w_hi, act_hi), (w_lo, act_hi), (w_hi, act_lo))):
                            mm = pe.matmul(bank[PLACE[("dn", m)][0]][:, 0:T], w[:, k % 4, P * m:P * m + P],
                                           x[k // 2][:, at:at + T], start=(k == 0 and which == 0), stop=(k == FC - 1 and which == 2))
                            if not (k == FC - 1 and which == 2):
                                tell(mm)
                    if i == 5:
                        filled(mm, ("dn", m))
                freed.append(S["pair_used"])
            freed.clear()
            norm_sum(("nfin", 0), sq)
            pe.wait_ge(S["normed"], NORMS["nfin"] + 8)
            for t in range(TT):
                for half in range(2):
                    turn(("out", 2 * t + half), [(c * P, hT[:, (4 * half + c) * T + t * P:][:, 0:P]) for c in range(4)])

        @block.scalar
        def _(act):
            act.dma_start(ch(att, 0, TT, D), A["x"][0].rearrange("(t p) d -> p t d", p=P)).then_inc(S["x_in"], 16)
            act.dma_start(w_f[:, :].rearrange("p (k n) -> p k n", k=DC), w_in2[:, :, 2304:2308]).then_inc(S["wf_in"], 16)

            def move(use, dst, src_n, func=ACT.Copy, scale=1.0, rows=slice(0, P)):
                b = arrive(act, use)
                emptied(act.activation(dst, b[rows, 0:src_n], func, scale=scale), use)

            def square(src, dst, words):
                for i in range(2):
                    h = words // 2
                    signal(act.activation(dst[:, i * h:i * h + h], src[:, i * h:i * h + h], ACT.Square), "squares")

            def square_residual(use, dst, before=None):
                for i in range(2):
                    for m in range(4 * i, 4 * i + 4):
                        copied(act, (use, m))
                    signal(act.activation(dst[:, 1024 * i:1024 * i + 1024], xT[:, 1024 * i:1024 * i + 1024], ACT.Square), "squares")

            def root(use):
                w, n = {u: (w, n) for u, w, n in ROOTS}[use]
                i = [u for u, _, _ in ROOTS].index(use)
                if i >= 2:
                    act.wait_ge(*[(S["normed"], 8), *((S["qk_ready"], k) for k in (1, 2, 3, 4)),
                                  (S["conv_z"], 4), (S["attn_out"], 1), (S["attn_out"], 2),
                                  *((S["normed"], k) for k in (16, 24, 32, 40, 48))][i - 2])
                b = arrive(act, use)
                emptied(act.activation(rs2[TURN[use]][:, 0:w], b[:, 0:w], ACT.Sqrt, bias=EPS, scale=1.0 / n), use)

            def exps(use, i, base, scale):
                act.wait_ge(S["s_max"], i + 1)
                s8 = 8 * (i % 8)
                for c in range(2):
                    e = item(base)[:, c * T:c * T + T]
                    signal(act.activation(e, e, ACT.Exp, bias=st[:, s8 + 2 + c:s8 + 3 + c], scale=scale,
                                          accum_out=st[:, s8 + 4 + c:s8 + 5 + c]), "s_exp")

            for i in range(4):
                move(("xT", i), xT[:, 512 * i:512 * i + 512], 512)
            for i in range(4):
                copied(act, ("xT", i))
            square(xT, sq, DC * T)
            def round_w_in(u):
                if u >= 2:
                    arrive(act, IN_LAST[u - 2])
                round_unit(act, "in", u)

            def gates(u):
                for m in range(4 * u, 4 * u + 4):
                    move(("gt", m), big[:, m * T:m * T + T], T, ACT.Sigmoid)

            root(("n1", 0))
            round_w_in(0)
            for i, dst in enumerate((parts["qko"][:, 2048:3072], parts["mrg"][:, 1024:2048])):
                act.wait_ge(S["normed"], 4 * i + 4)
                signal(act.activation(dst, hT[:, 1024 * i:1024 * i + 1024], ACT.Copy), "h1_hi")
            move(("lam", 0), st[:, 102:104], 2, ACT.Exp)
            round_w_in(1)
            round_w_in(2)
            for m in range(4):
                move(("cg", m), mrg[:, m * T:m * T + T], T, ACT.Sigmoid)
            for at, use in enumerate("qk"):
                round_w_in(3 + at)
                for m in range(4):
                    move((use, m), qko[:, (4 * at + m) * T:(4 * at + m + 1) * T], T)
                for m in range(4):
                    copied(act, (use, m))
                square(qko[:, 1024 * at:1024 * at + 1024], sq[:, 1024 * at:1024 * at + 1024], 1024)
            round_w_in(5)
            for t in range(TT):
                move(("v", t), vtok[:, 512 * t:512 * t + 512], 512)
            round_w_in(6)
            for use in ("qn", "kn"):
                for i in range(2):
                    root((use, i))
            gates(0)
            round_w_in(7)
            gates(1)
            round_w_in(8)
            for i in range(4):
                exps("s1", i, 512 * i, 0.125)
            act.wait_ge(S["conv_dev"], 1)
            square(big[:, 16 * T:20 * T], sq[:, 1024:2048], 1024)
            for i in range(4, 8):
                exps("s1", i, 512 * i, 0.125)
            gates(2)
            root(("var", 0))
            act.wait_ge(S["conv_z"], 4)
            signal(act.activation(sq[:, 1024:2048], big[:, 16 * T:20 * T], ACT.Sigmoid), "conv_sig")
            gates(3)
            act.wait_ge(S["conv_out"], 1)
            for h in range(4):
                move(("aT1", h), sq[:, 512 * h:512 * h + 512], 512)
            for h in range(4):
                move(("o1", h), qko[:, (8 + h) * T:(9 + h) * T], T)
            act.dma_start(att[:, 2048:4096].rearrange("p (t d) -> p t d", t=TT),
                          A["mem_2"][0].rearrange("(t p) d -> p t d", p=P)).then_inc(S["mem_in"], 16)
            for h in range(4):
                copied(act, ("o1", h))
            square(qko[:, 2048:3072], sq[:, 0:1024], 1024)
            root(("on", 0))
            root(("on", 1))
            for i in range(4):
                move(("mT", i), qko[:, 512 * i:512 * i + 512], 512)
            for i in range(4):
                copied(act, ("mT", i))
            act.wait_ge(S["merged"], 8)
            square(qko[:, 0:2048], big[:, 0:2048], DC * T)
            root(("nmem", 0))
            square_residual("wo", sq)
            for m in range(2):
                move(("kx", m), att[:, (8 + m) * T:(9 + m) * T], T)
            root(("n2", 0))
            for m in range(2, 4):
                move(("kx", m), att[:, (8 + m) * T:(9 + m) * T], T)
            for t in range(TT):
                for half in range(2):
                    move(("h2t", 2 * t + half), att[:, t * D + half * 512:t * D + half * 512 + 512], 512)
            act.wait_ge(S["logits"], 1)
            signal(act.activation(g_gap, g_gap, ACT.Exp), "g_exp")
            act.dma_start(pos_i, A["positions_2"]).then_inc(S["pos_in"], 16)
            act.wait_ge(S["pair_gap"], 1)
            signal(act.activation(e_gap, e_gap, ACT.Exp), "e_exp")
            for m in range(4, 8):
                move(("kx", m), att[:, (8 + m) * T:(9 + m) * T], T)
            act.wait_ge(S["rounds"], 1)
            steps = act.value_load(count_i[0:1, 0:1], min_val=QUADS, max_val=QUADS * ROUNDS)
            act.sem_inc(S["y_out"], 1)
            with act.Fori(0, steps) as n:
                act.wait_ge(S["swt_full"], n + 1)
                act.activation(swT, bank[4][:, 0:T], ACT.Copy).then_inc(S["swt"], 1)
                for i in range(2):
                    act.wait_ge(S["rows_full"], n * 2 + i + 2)
                    act.activation(xeT[:, 4 * i:4 * i + 4].rearrange("p k s -> p (k s)"), bank[5 + i][:, :],
                                   ACT.Copy).then_inc(S["rows"], 1)
                i = PRE_UNITS + 3
                act.wait_ge(used[i % RING], n * 2 + i // RING + 1)
                act.activation(sig, bank[0][:, :], ACT.Sigmoid).then_inc(S["gate_sig"], 1)
                act.wait_ge(S["hid_full"], n + 1)
                act.activation(hidT.rearrange("p k s -> p (k s)"), bank[7][:, :], ACT.Copy).then_inc(S["hidT"], 1)
                i = PRE_UNITS + 11
                act.wait_ge(used[i % RING], n * 2 + i // RING + 1)
                for i in range(2):
                    act.activation(y_e[:, 512 * i:512 * i + 512], bank[2 + i][:, :], ACT.Copy).then_inc(S["y_out"], 1)

            act.wait_ge(S["experts_done"], 1)
            square(xT, sq, DC * T)
            root(("nmix", 0))
            act.wait_ge(S["ang"], 2)
            signal(act.activation(pad[:, 0:512], pad[:, 0:512], ACT.Sin), "trig")
            def mem_values(u):
                for t in range(TT):
                    move(("vx", 2 * u + t), mrg[:, t * 1024 + u * 512:t * 1024 + u * 512 + 512], 512)

            mem_values(0)
            for m in (4, 5):
                move(("pa", m), big[:, m * T:m * T + T], T)
            for at, use in ((6, "qb"), (8, "kb")):
                for m in range(2):
                    move((use, m), big[:, (at + m) * T:(at + m + 1) * T], T)
            for t in range(TT):
                move(("vb", t), vtok[:, 512 * t:512 * t + 256], 256)
            for m in range(2):
                b = arrive(act, ("qc", m))
                signal(act.activation(qc_head[2 * m], b[:, 0:T], ACT.Copy, scale=C("eighth")[:, 0:1]), "act_step")
                emptied(act.activation(qc_head[2 * m + 1], b[:, 0:T], ACT.Copy, scale=C("eighth")[:, 1:2]), ("qc", m))
            for m in range(2):
                move(("kc", m), big[:, (12 + m) * T:(13 + m) * T], T)
            act.wait_ge(S["f_abs"], 1)
            signal(act.activation(f_e, f_abs, ACT.Exp, scale=-1.0), "f_exp")
            act.wait_ge(S["f_exp"], 1)
            signal(act.activation(f_e, f_e, ACT.Ln, bias=1.0), "f_exp")
            for i in range(4):
                exps("sb", 8 + i, 512 * i, 0.125)
            mem_values(1)
            for i in range(4):
                exps("sc", 12 + i, FORGET + 512 * i, 1.0)
            def round_weights(u):
                if u < len(FF_FREE):
                    arrive(act, FF_FREE[u])
                else:
                    act.wait_ge(S["pair_used"], u - FIRST_DN - 1)
                round_unit(act, "ff", u)

            def round_input(dst, src, ready):
                for i in range(2):
                    ready(i)
                    signal(act.activation(dst[:, 1024 * i:1024 * i + 1024], src[:, 1024 * i:1024 * i + 1024], ACT.Copy), "x_hi")

            round_weights(0)
            for t in range(TT):
                move(("vc", t), vtok[:, 512 * t + 256:512 * t + 512], 256)
            act.wait_ge(S["rows_zero"], 1)
            for m in range(2):
                move(("pd", m), pool_x[:, m, 16:16 + T], T)
            for m in range(4):
                move(("pa", m), big[:, m * T:m * T + T], T)
            for name, base, at in (("b", 0, 2), ("c", FORGET, 4)):
                for h in range(4):
                    move(("aT" + name, h), item(base + 512 * h), 512)
                for h2 in range(2):
                    move(("o" + name, h2), hT[:, (at + h2) * T:(at + h2 + 1) * T], T)
                if name == "b":
                    round_weights(1)

            def mixed(i):
                act.wait_ge(S["y_mix"], 4 if i else 2)
                for h2 in range(2):
                    copied(act, (("ob", "oc")[i], h2))

            def normed_xa(i):
                act.wait_ge(S["normed"], NORMS["nxa"] + 4 * i + 4)

            def crossed(i):
                for h in (2 * i, 2 * i + 1):
                    copied(act, ("ox", h))

            round_input(parts["big"], hT, mixed)
            round_weights(2)
            square_residual("w2", sq)
            root(("nxa", 0))
            round_input(parts["big"][:, 2048:4096], hT, normed_xa)
            round_weights(3)
            for u in range(2):
                for m in range(4 * u, 4 * u + 4):
                    move(("qx", m), qko[:, m * T:m * T + T], T)
                for i in (2 * u, 2 * u + 1):
                    exps("sx", 16 + i, 512 * i, 1.0 / 16)
                if u == 0:
                    round_weights(4)
            for h in range(4):
                move(("aTx", h), sq[:, 512 * h:512 * h + 512], 512)
            round_weights(5)
            for h in range(4):
                move(("ox", h), big[:, 512 * h:512 * h + 512], 512)
            round_input(parts["hT"], big, crossed)

            def gate(i):
                act.wait_ge(S["up_conv"], i + 1)
                signal(act.activation(up_s, up_ys[i % 2][:, 512:1024], ACT.Sigmoid), "up_sig")

            def round_act(i):
                act.wait_ge(S["up_val"], i + 1)
                signal(act.activation(act_hi[i], up_vals[i % 2], ACT.Copy), "act_hi")

            round_weights(6)
            square_residual("xo", sq)
            root(("nffn", 0))
            for i in range(2):
                act.wait_ge(S["normed"], NORMS["nffn"] + 4 * i + 4)
                signal(act.activation(h_hi[:, 1024 * i:1024 * i + 1024], hT[:, 1024 * i:1024 * i + 1024], ACT.Copy), "h_hi")
            round_weights(7)
            act.wait_ge(S["pads_zero"], 1)
            for i in range(11):
                if i < 10:
                    round_weights(i + 8)
                if i:
                    gate(i - 1)
                up_y = up_ys[i % 2]
                for a, use in enumerate(("ua", "ug")):
                    b = arrive(act, (use, i))
                    for c in range(2):
                        q = 2 * a + c
                        signal(act.activation(up_y[:, q * T:q * T + T], b[:, c * T:c * T + T], ACT.Copy,
                                              scale=col("ff_taps", 3 * (2 * i + c + FC * a) + 2)), "act_step")
                    emptied(act.activation(up_x[:, 2 * a:2 * a + 2, 2:2 + T], b[:, :].rearrange("p (c t) -> p c t", c=2),
                                           ACT.Copy), (use, i))
                if i:
                    round_act(i - 1)
            round_weights(18)
            gate(10)
            round_act(10)
            for u in range(19, len(ffn)):
                round_weights(u)
            square_residual("dn", sq)
            root(("nfin", 0))
            for i in range(4):
                move(("out", i), att[:, 512 * i:512 * i + 512], 512)

        @block.vector
        def _(dve):
            def step(ins):
                done(dve, ins, "dve_step")

            def inverse_root(use):
                w = {u: w for u, w, _ in ROOTS}[use]
                copied(dve, use)
                r = rs2[TURN[use]][:, 0:w]
                step(dve.reciprocal(r, r))
                return r

            def normalise(use, g, src, dst):
                r = inverse_root(use)
                for c in range(DC):
                    signal(dve.scalar_tensor_tensor(out=dst[:, c * T:c * T + T], in0=src[:, c * T:c * T + T],
                                                    scalar=col(g, c), in1=r, op0=ALU.mult, op1=ALU.mult), "normed")

            def maxima(use, i, base, scale, mask=None):
                b = arrive(dve, use)
                s = item(base)
                if mask is None:
                    ins = dve.tensor_copy(s, b[:, :])
                else:
                    ins = dve.tensor_tensor(s, b[:, :], C(mask), ALU.add)
                emptied(ins, use)
                copied(dve, use)
                s8 = 8 * (i % 8)
                step(dve.tensor_reduce(st[:, s8:s8 + 2], s.rearrange("p (t k) -> p t k", t=TT), AX, ALU.max))
                signal(dve.tensor_scalar(st[:, s8 + 2:s8 + 4], st[:, s8:s8 + 2], -scale, None, ALU.mult), "s_max")

            def shares(i, base, mult=None):
                dve.wait_ge(S["s_exp"], 2 * i + 2)
                s8 = 8 * (i % 8)
                s = item(base).rearrange("p (t k) -> p t k", t=TT)
                if mult is not None:
                    step(dve.tensor_tensor(s, s, C(mult).rearrange("p (t k) -> p t k", t=TT), ALU.mult))
                    step(dve.tensor_reduce(st[:, s8 + 4:s8 + 6], s, AX, ALU.add))
                step(dve.reciprocal(st[:, s8 + 6:s8 + 8], st[:, s8 + 4:s8 + 6]))
                signal(dve.tensor_tensor(s, s, st[:, s8 + 6:s8 + 8].unsqueeze(2).broadcast_to([P, TT, T]), ALU.mult), "a_ready")

            dve.wait_ge(S["const_in"], 16)
            dve.wait_ge(S["par_in"], 16)
            step(dve.memset(st[:, :], 0.0))
            step(dve.tensor_tensor(st[:, 98:99], W("lam_q"), W("lam_k"), ALU.mult))
            signal(dve.tensor_scalar(st[:, 100:102], C("halves"), st[:, 98:99], None, ALU.mult), "lam_in")
            for i in range(4):
                copied(dve, ("xT", i))
            normalise(("n1", 0), "g1", xT, hT)
            rest_of_unit(dve, "in", 0, 1, "in_lo_first")
            for i, hi in enumerate((parts["qko"][:, 2048:3072], parts["mrg"][:, 1024:2048])):
                dve.wait_ge(S["h1_hi"], i + 1)
                part = slice(1024 * i, 1024 * i + 1024)
                signal(dve.tensor_tensor(h1_lo[:, part], hT[:, part], hi.bitcast(F32), ALU.subtract), "h1_lo")
            copied(dve, ("lam", 0))
            step(dve.tensor_tensor(st[:, 104:105], st[:, 103:104], st[:, 102:103], ALU.subtract))
            step(dve.tensor_scalar(st[:, 104:105], st[:, 104:105], -LAM0, None, ALU.add))
            step(dve.tensor_scalar(st[:, 105:106], W("sub_g"), 1.0 - LAM0, None, ALU.mult))
            dve.wait_ge(S["zeroed"], 1)
            rows = pad[:, :].rearrange("p (c t) -> p c t", c=4)
            for m in range(4):
                b = arrive(dve, ("ca", m))
                copied(dve, ("cg", m))
                emptied(dve.tensor_tensor(rows[:, m, CW - 1:], b[:, 0:T], mrg[:, m * T:m * T + T], ALU.mult), ("ca", m))
            for m in range(4):
                copied(dve, ("ca", m))

            def convolve(ms, between=None):
                y = {m: big[:, (16 + m) * T:(17 + m) * T] for m in ms}
                last = {m: signal(dve.tensor_scalar(y[m], rows[:, m, 0:T], col("taps", CW * m), col("conv_b", m),
                                                    ALU.mult, ALU.add), "dve_step") for m in ms}
                for j in range(1, CW):
                    if j == CW // 2 and between:
                        between()
                    for m in ms:
                        dve.wait_ge(S["dve_step"], last[m])
                        ins = dve.scalar_tensor_tensor(out=y[m], in0=rows[:, m, j:j + T], scalar=col("taps", CW * m + j), in1=y[m],
                                                       op0=ALU.mult, op1=ALU.add)
                        last[m] = signal(ins, "dve_step" if j < CW - 1 else "conved")

            def queries_and_keys():
                for at, use in enumerate(("qn", "kn")):
                    for i in range(2):
                        r = inverse_root((use, i))
                        x = qko[:, 1024 * at + 512 * i:1024 * at + 512 * i + 512]
                        signal(dve.scalar_tensor_tensor(out=x, in0=x, scalar=col(("q_g", "k_g")[at], 0), in1=r,
                                                        op0=ALU.mult, op1=ALU.mult), "qk_ready")

            convolve((0, 1))
            convolve((2, 3), queries_and_keys)
            for i in range(4):
                maxima(("s1", i), i, 512 * i, 0.125, "causal")
            y4 = big[:, 16 * T:20 * T].rearrange("p (c t) -> p c t", c=4)
            b = arrive(dve, ("mu", 0))
            emptied(dve.tensor_scalar(mean_row, b[:, 0:T], 1.0 / 512, None, ALU.mult), ("mu", 0))
            copied(dve, ("mu", 0))
            dve.wait_ge(S["conved"], 4)
            signal(dve.tensor_tensor(y4, y4, mean_row.unsqueeze(1).broadcast_to([P, 4, T]), ALU.subtract), "conv_dev")

            def differences(h):
                dve.wait_ge(S["s_exp"], 4 * h + 4)
                s0, s1 = 16 * h, 16 * h + 8
                step(dve.reciprocal(st[:, s0 + 6:s0 + 8], st[:, s0 + 4:s0 + 6]))
                step(dve.reciprocal(st[:, s1 + 6:s1 + 8], st[:, s1 + 4:s1 + 6]))
                for t in range(TT):
                    e0, e1 = (att[:, 1024 * h + 512 * c + T * t:][:, 0:T] for c in range(2))
                    step(dve.tensor_scalar(e1, e1, st[:, s1 + 6 + t:s1 + 7 + t], st[:, 104:105], ALU.mult, ALU.mult))
                    signal(dve.scalar_tensor_tensor(out=e0, in0=e0, scalar=st[:, s0 + 6 + t:s0 + 7 + t], in1=e1,
                                                    op0=ALU.mult, op1=ALU.add), "a_ready")

            for i in range(4, 8):
                maxima(("s1", i), i, 512 * i, 0.125, "causal")
            for h in range(2):
                differences(h)
            r = inverse_root(("var", 0))
            dve.wait_ge(S["conv_dev"], 1)
            step(dve.tensor_tensor(y4, y4, r.unsqueeze(1).broadcast_to([P, 4, T]), ALU.mult))
            for m in range(4):
                signal(dve.tensor_scalar(y4[:, m], y4[:, m], col("ln_g", m), col("ln_b", m), ALU.mult, ALU.add), "conv_z")
            dve.wait_ge(S["conv_z"], 4)
            dve.wait_ge(S["conv_sig"], 1)
            signal(dve.tensor_tensor(big[:, 16 * T:20 * T], big[:, 16 * T:20 * T], sq[:, 1024:2048], ALU.mult), "conv_out")
            for h in range(2, 4):
                differences(h)
            for m in range(8):
                b = arrive(dve, ("co", m))
                copied(dve, ("gt", m))
                emptied(dve.tensor_tensor(mrg[:, m * T:m * T + T], b[:, 0:T], big[:, m * T:m * T + T], ALU.mult), ("co", m))
            for i in range(2):
                r = inverse_root(("on", i))
                x = qko[:, 2048 + 512 * i:2560 + 512 * i]
                for h in range(2):
                    copied(dve, ("o1", 2 * i + h))
                signal(dve.scalar_tensor_tensor(out=x, in0=x, scalar=st[:, 105:106], in1=r,
                                                op0=ALU.mult, op1=ALU.mult), "attn_out")
            for m in range(8):
                b = arrive(dve, ("ao", m))
                copied(dve, ("gt", 8 + m))
                g = big[:, (8 + m) * T:(9 + m) * T]
                emptied(dve.tensor_tensor(g, b[:, 0:T], g, ALU.mult), ("ao", m))
                copied(dve, ("ao", m))
                copied(dve, ("co", m))
                y = mrg[:, m * T:m * T + T]
                signal(dve.tensor_tensor(y, y, g, ALU.add), "merged")

            def residual(use, n=8):
                for m in range(n):
                    b = arrive(dve, (use, m))
                    x = xT[:, m * T:m * T + T]
                    emptied(dve.tensor_tensor(x, b[:, 0:T], x, ALU.add), (use, m))
                for m in range(n):
                    copied(dve, (use, m))

            normalise(("nmem", 0), "g_mem", qko, qko)
            residual("wo")
            normalise(("n2", 0), "g2", xT, hT)
            for t in range(TT):
                b = arrive(dve, ("rt", t))
                emptied(dve.tensor_copy(logit[:, t], b[:, 0:36]), ("rt", t))
            for t in range(TT):
                copied(dve, ("rt", t))
            lg = logit[:, :, 0:NG]
            le = logit[:, :, NG:36].rearrange("p t (g j) -> p t g j", g=NG)

            def first_max(values, n, best, one_hot, tmp):
                fall = C("falling")[:, 0:n].unsqueeze(1).broadcast_to([P, TT, n])
                step(dve.tensor_reduce(best, values, AX, ALU.max))
                step(dve.tensor_tensor(tmp, values, best.unsqueeze(2).broadcast_to([P, TT, n]), ALU.is_equal))
                step(dve.tensor_tensor(tmp, tmp, fall, ALU.mult))
                step(dve.tensor_reduce(tie, tmp, AX, ALU.max))
                step(dve.tensor_tensor(one_hot, tmp, tie.unsqueeze(2).broadcast_to([P, TT, n]), ALU.is_equal))

            first_max(lg, NG, g_max, g_hot, g_tmp)
            signal(dve.tensor_tensor(g_gap3, lg, g_max.unsqueeze(2).broadcast_to([P, TT, NG]), ALU.subtract), "logits")
            hot4 = g_hot.unsqueeze(3).broadcast_to([P, TT, NG, EG])
            for t in range(TT):
                step(dve.tensor_tensor(e_all[:, t], le[:, t], hot4[:, t], ALU.mult))
            step(dve.tensor_reduce(e_val, e_all.rearrange("p t g j -> p t j g"), AX, ALU.add))
            first_max(e_val, EG, e_max1, hot1, e_tmp)
            step(dve.scalar_tensor_tensor(out=e_val, in0=hot1, scalar=-BIG, in1=e_val, op0=ALU.mult, op1=ALU.add))
            first_max(e_val, EG, e_max2, hot2, e_tmp)
            signal(dve.tensor_tensor(e_gap, e_max2, e_max1, ALU.subtract), "pair_gap")
            step(dve.tensor_tensor(e_tmp, hot1, hot2, ALU.add))
            for t in range(TT):
                step(dve.tensor_tensor(member[:, t], hot4[:, t], e_tmp[:, t].unsqueeze(1).broadcast_to([P, NG, EG]), ALU.mult))
            signal(dve.memset(tie, 0.0), "member")
            dve.wait_ge(S["g_exp"], 1)
            step(dve.tensor_reduce(g_sum, g_gap3, AX, ALU.add))
            dve.wait_ge(S["e_exp"], 1)
            step(dve.scalar_tensor_tensor(out=g_sum, in0=e_gap, scalar=1.0, in1=g_sum, op0=ALU.add, op1=ALU.mult))
            step(dve.reciprocal(w_1, g_sum))
            step(dve.tensor_tensor(w_2, w_1, e_gap, ALU.mult))
            step(dve.tensor_tensor(hot1, hot1, w_1.unsqueeze(2).broadcast_to([P, TT, EG]), ALU.mult))
            step(dve.tensor_tensor(hot2, hot2, w_2.unsqueeze(2).broadcast_to([P, TT, EG]), ALU.mult))
            step(dve.tensor_tensor(hot1, hot1, hot2, ALU.add))
            for t in range(TT):
                step(dve.tensor_tensor(e_all[:, t], hot4[:, t], hot1[:, t].unsqueeze(1).broadcast_to([P, NG, EG]), ALU.mult))
            for t in range(TT):
                b = arrive(dve, ("pos", t))
                mt = member[:, t].rearrange("p g j -> p (g j)")
                q = place_of[:, t]
                emptied(dve.scalar_tensor_tensor(out=q, in0=b[:, 0:NE], scalar=1.0, in1=mt, op0=ALU.add, op1=ALU.mult), ("pos", t))
                copied(dve, ("pos", t))
                step(dve.tensor_scalar(q, q, -1.0, None, ALU.add))
                so = slot_of[:, t].rearrange("p (r e) -> p r e", r=ROUNDS)
                step(dve.tensor_tensor(so, q.unsqueeze(1).broadcast_to([P, ROUNDS, NE]),
                                       C("round_start").unsqueeze(2).broadcast_to([P, ROUNDS, NE]), ALU.subtract))
                wo = weight_of[:, t].rearrange("p (r e) -> p r e", r=ROUNDS)
                step(dve.tensor_copy(wo, e_all[:, t].rearrange("p g j -> p (g j)").unsqueeze(1).broadcast_to([P, ROUNDS, NE])))
            b = arrive(dve, ("cnt", 0))
            emptied(dve.tensor_reduce(st[:, 106:107], b[:, 0:NE], AX, ALU.max), ("cnt", 0))
            copied(dve, ("cnt", 0))
            step(dve.tensor_tensor(st[:, 108:116], st[:, 106:107].broadcast_to([P, ROUNDS]), C("round_start"), ALU.is_gt))
            step(dve.tensor_reduce(st[:, 107:108], st[:, 108:116], AX, ALU.add))
            signal(dve.tensor_scalar(count_i[:, :], st[:, 107:108], float(QUADS), None, ALU.mult), "rounds")
            dve.wait_ge(S["rounds"], 1)
            steps = dve.value_load(count_i[0:1, 0:1], min_val=QUADS, max_val=QUADS * ROUNDS)
            iota = C("iota").unsqueeze(1).broadcast_to([P, QUAD, CAP])
            dve.sem_inc(S["hidden"], 1)
            dve.sem_inc(S["added"], 1)
            with dve.Fori(0, steps) as n:
                dve.wait_ge(S["rows_full"], n * 2 + 1)
                dve.wait_ge(S["added"], n * 4 + 1)
                for t in range(TT):
                    here = slot_of[:, t, bass.ds(n * QUAD, QUAD)].unsqueeze(2).broadcast_to([P, QUAD, CAP])
                    dve.tensor_tensor(pick[:, t], here, iota, ALU.is_equal).then_inc(S["pick_step"], 1)
                dve.wait_ge(S["pick_step"], n * 2 + 2)
                for t in range(TT):
                    wt = weight_of[:, t, bass.ds(n * QUAD, QUAD)].unsqueeze(2).broadcast_to([P, QUAD, CAP])
                    dve.tensor_tensor(wpick[:, t], pick[:, t], wt, ALU.mult).then_inc(S["picked"], 1)
                dve.wait_ge(S["gate_sig"], n + 1)
                dve.tensor_tensor(sig, bank[0][:, :], sig, ALU.mult).then_inc(S["hid_step"], 1)
                dve.wait_ge(S["hid_step"], n + 1)
                i = PRE_UNITS + 7
                dve.wait_ge(used[i % RING], n * 2 + i // RING + 1)
                dve.tensor_tensor(hid, bank[1][:, :], sig, ALU.mult).then_inc(S["hidden"], 1)
                for i in range(4):
                    dve.wait_ge(S["comb_full"], n * 4 + i + 1)
                    x = xT[:, 512 * i:512 * i + 512]
                    dve.tensor_tensor(x, bank[4 + i][:, :], x, ALU.add).then_inc(S["added"], 1)

            done(dve, dve.memset(st[:, :], 0.0), "experts_done")
            dve.wait_ge(S["pos_in"], 16)
            signal(dve.tensor_copy(st_pos[0:1, :], pos_i), "pos_f")
            b = arrive(dve, ("posb", 0))
            ang, turns = att[:, 0:T], att[:, T:2 * T]
            emptied(dve.tensor_scalar(ang, b[:, 0:T], C("inv_freq"), None, ALU.mult), ("posb", 0))
            copied(dve, ("posb", 0))
            step(dve.tensor_scalar(turns, ang, 1.0 / (2 * np.pi), None, ALU.mult))
            step(dve.tensor_scalar(turns, turns, MAGIC, None, ALU.add))
            step(dve.tensor_scalar(turns, turns, -MAGIC, None, ALU.add))
            for part in TWO_PI:
                step(dve.scalar_tensor_tensor(out=ang, in0=turns, scalar=-part, in1=ang, op0=ALU.mult, op1=ALU.add))
            lim = 3.1415925
            signal(dve.tensor_scalar(pad[:, T:2 * T], ang, lim, -lim, ALU.min, ALU.max), "ang")
            step(dve.tensor_scalar(ang, ang, np.pi / 2, None, ALU.add))
            step(dve.tensor_scalar(turns, ang, lim, -2 * np.pi, ALU.is_gt, ALU.mult))
            step(dve.tensor_tensor(ang, ang, turns, ALU.add))
            signal(dve.tensor_scalar(pad[:, 0:T], ang, lim, -lim, ALU.min, ALU.max), "ang")
            normalise(("nmix", 0), "g_mix", xT, hT)
            step(dve.memset(conv_x, 0.0))
            step(dve.memset(c_rows, 0.0))
            step(dve.memset(f_zero, 0.0))
            dve.wait_ge(S["trig"], 1)
            for use, at in (("rq", 6), ("rk", 8)):
                b = arrive(dve, (use, 0))
                x = ch(big, at, 2)
                cos = pad[:, 0:T].unsqueeze(1).broadcast_to([P, 2, T])
                sin = pad[:, T:2 * T].unsqueeze(1).broadcast_to([P, 2, T])
                r3 = rs2[1][:, :].rearrange("p (c t) -> p c t", c=2)
                emptied(dve.tensor_tensor(r3, b[:, :].rearrange("p (c t) -> p c t", c=2), sin, ALU.mult), (use, 0))
                copied(dve, (use, 0))
                step(dve.tensor_tensor(x, x, cos, ALU.mult))
                done(dve, dve.tensor_tensor(x, x, r3, ALU.add), "rope")
            b = arrive(dve, ("f", 0))
            emptied(dve.tensor_scalar(f_z, b[0:4, 0:T], col("b_f", 0, slice(0, 4)), None, ALU.add), ("f", 0))
            copied(dve, ("f", 0))
            step(dve.tensor_scalar(f_abs, f_z, -1.0, None, ALU.mult))
            signal(dve.tensor_tensor(f_abs, f_abs, f_z, ALU.max), "f_abs")
            step(dve.tensor_scalar(f_z, f_z, 0.0, None, ALU.min))
            dve.wait_ge(S["f_exp"], 2)
            step(dve.tensor_tensor(f_z, f_z, f_e, ALU.subtract))
            signal(dve.tensor_tensor_scan(c_row[0:4], f_z, f_zero, 0.0, ALU.add, ALU.add), "c_rows")
            dve.wait_ge(S["c_rows"], 1)
            signal(dve.tensor_scalar(neg_c[0:4], c_row[0:4], -1.0, None, ALU.mult), "c_rows")
            for i in range(4):
                maxima(("sb", i), 8 + i, 512 * i, 0.125, "dil_mask")
            for i in range(4):
                maxima(("sc", i), 12 + i, FORGET + 512 * i, 1.0, "causal")
            for i in range(4):
                copied(dve, ("vx", i))
            signal(dve.memset(pool_x, 0.0), "rows_zero")
            for i in range(4):
                shares(8 + i, 512 * i, "dil_mult")
            for m in range(2):
                copied(dve, ("pd", m))
            width = 16 + T
            step(dve.tensor_copy(pool_s[0][:, :, 0:1], pool_x[:, :, 0:1]))
            step(dve.tensor_tensor(pool_s[0][:, :, 1:], pool_x[:, :, 1:], pool_x[:, :, :width - 1], ALU.add))
            step(dve.tensor_copy(pool_s[1][:, :, 0:2], pool_s[0][:, :, 0:2]))
            step(dve.tensor_tensor(pool_s[1][:, :, 2:], pool_s[0][:, :, 2:], pool_s[0][:, :, :width - 2], ALU.add))
            z = z_pool.rearrange("p (c t) -> p c t", c=2)
            step(dve.tensor_copy(z[0:64, 0], pool_s[0][0:64, 0, 16:]))
            step(dve.tensor_copy(z[64:128, 0], pool_s[1][64:128, 0, 16:]))
            a8, a16 = pool_s[0][:, 1], pool_s[0][:, 0]
            step(dve.tensor_copy(a8[:, 0:4], pool_s[1][:, 1, 0:4]))
            step(dve.tensor_tensor(a8[:, 4:], pool_s[1][:, 1, 4:], pool_s[1][:, 1, :width - 4], ALU.add))
            step(dve.tensor_tensor(a16[:, 8:], a8[:, 8:], a8[:, :width - 8], ALU.add))
            step(dve.tensor_copy(z[0:64, 1], a8[0:64, 16:]))
            step(dve.tensor_copy(z[64:128, 1], a16[64:128, 16:]))
            step(dve.tensor_tensor(z_pool, z_pool, C("inv_count"), ALU.mult))
            signal(dve.tensor_tensor(z, z, pool_x[:, :, 16:], ALU.subtract), "z_pool")
            for i in range(4):
                shares(12 + i, FORGET + 512 * i)
            for m in range(6):
                copied(dve, ("pa", m))
            step(dve.tensor_tensor(conv_x[:, :, 2:], ch(big, 4, 2), ch(big, 0, 2), ALU.mult))
            for c in range(2):
                y = hT[:, c * T:c * T + T]
                step(dve.tensor_scalar(y, conv_x[:, c, 0:T], col("w_sc", 3 * c), None, ALU.mult))
                for j in range(1, 3):
                    step(dve.scalar_tensor_tensor(out=y, in0=conv_x[:, c, j:j + T], scalar=col("w_sc", 3 * c + j), in1=y,
                                                  op0=ALU.mult, op1=ALU.add))
                signal(dve.tensor_tensor(y, y, ch(big, 2 + c), ALU.mult), "y_mix")
            rest_of_unit(dve, "ff", 0, 1, "ff_lo_dve")
            b = arrive(dve, ("pl", 0))
            signal(dve.tensor_scalar(hT[:, 6 * T:7 * T], b[:, 0:T], col("pool_g", 0), None, ALU.mult), "y_mix")
            emptied(dve.tensor_scalar(hT[:, 7 * T:8 * T], b[:, T:2 * T], col("pool_g", 1), None, ALU.mult), ("pl", 0))
            copied(dve, ("pl", 0))
            signal(dve.memset(st[:, 120:121], 0.0), "y_mix")
            def rest_of_input(stage, dst, src, hi):
                for i in range(2):
                    dve.wait_ge(S["x_hi"], 2 * stage + i + 1)
                    part = slice(1024 * i, 1024 * i + 1024)
                    signal(dve.tensor_tensor(dst[:, part], src[:, part], hi[:, part].bitcast(F32), ALU.subtract), "x_lo")

            rest_of_unit(dve, "ff", 1, 1, "ff_lo_dve")
            rest_of_input(0, parts["hT"], hT, parts["big"])
            rest_of_unit(dve, "ff", 2, 1, "ff_lo_dve")
            residual("w2")
            normalise(("nxa", 0), "g_xa", xT, hT)
            rest_of_input(1, parts["hT"], hT, parts["big"][:, 2048:4096])
            rest_of_unit(dve, "ff", 3, 1, "ff_lo_dve")
            for u in range(2):
                for i in (2 * u, 2 * u + 1):
                    maxima(("sx", i), 16 + i, 512 * i, 1.0 / 16)
                for i in (2 * u, 2 * u + 1):
                    shares(16 + i, 512 * i)
                if u == 0:
                    rest_of_unit(dve, "ff", 4, 1, "ff_lo_dve")
            rest_of_unit(dve, "ff", 5, 1, "ff_lo_dve")
            rest_of_input(2, parts["big"], big, parts["hT"])

            def gated(i):
                y = up_ys[i % 2]
                step(dve.tensor_tensor(y[:, 0:512], y[:, 0:512], y[:, 512:1024], ALU.mult))
                dve.wait_ge(S["up_sig"], i + 1)
                signal(dve.tensor_tensor(up_vals[i % 2], y[:, 0:512], up_s, ALU.mult), "up_val")

            def rest_of_act(i):
                dve.wait_ge(S["act_hi"], i + 1)
                signal(dve.tensor_tensor(act_lo[i], up_vals[i % 2], act_hi[i].bitcast(F32), ALU.subtract), "act_lo")

            rest_of_unit(dve, "ff", 6, 1, "ff_lo_dve")
            residual("xo")
            signal(dve.memset(pad[:, :], 0.0), "pads_zero")
            normalise(("nffn", 0), "g_ffn", xT, hT)
            for i in range(2):
                dve.wait_ge(S["h_hi"], i + 1)
                part = slice(1024 * i, 1024 * i + 1024)
                signal(dve.tensor_tensor(h_lo[:, part], hT[:, part], h_hi[:, part].bitcast(F32), ALU.subtract), "h_lo")
            rest_of_unit(dve, "ff", 7, 1, "ff_lo_dve")
            for i in range(11):
                if i < 10:
                    rest_of_unit(dve, "ff", i + 8, 1, "ff_lo_dve")
                if i:
                    gated(i - 1)
                for a, use in enumerate(("ua", "ug")):
                    copied(dve, (use, i))
                up_y = up_ys[i % 2]
                for j in range(2):
                    for q in range(4):
                        chunk = 2 * i + q % 2 + FC * (q // 2)
                        y = up_y[:, q * T:q * T + T]
                        if j:
                            dve.wait_ge(S["dve_step"], count["dve_step"] - 3 + q)
                        ins = dve.scalar_tensor_tensor(out=y, in0=up_x[:, q, j:j + T], scalar=col("ff_taps", 3 * chunk + j),
                                                       in1=y, op0=ALU.mult, op1=ALU.add)
                        if (q, j) == (3, 1):
                            dve.wait_ge(S["up_conv"], signal(ins, "up_conv"))
                        elif j:
                            signal(ins, "up_tap")
                        else:
                            signal(ins, "dve_step")
                if i:
                    rest_of_act(i - 1)
            rest_of_unit(dve, "ff", 18, 1, "ff_lo_dve")
            gated(10)
            rest_of_act(10)
            for u in range(19, len(ffn)):
                rest_of_unit(dve, "ff", u, 1, "ff_lo_dve")
            residual("dn")
            normalise(("nfin", 0), "g_fin", xT, hT)


WEIGHTS = ["x", "w_in", "w_conv_out", "w_attn_out", "w_out", "w_gate_e", "w_up_e", "w_down_e", "mem_2", "positions_2",
           "w_in_2", "w_out_2", "w_xq_2", "w_xkv_2", "w_xo_2", "w_up_2", "w_down_2"]


def lay_out(inputs):
    at, n = param_places()
    par = np.zeros((P, n), np.float32)

    def put(name, a, rows=P):
        i, j = at[name]
        par[0:rows, i:j] = a

    def cols(a):
        return np.asarray(a).reshape(-1, P).T

    for name, key in (("g1", "attn_norm_g"), ("conv_b", "conv_dw_b"), ("ln_g", "conv_ln_g"), ("ln_b", "conv_ln_b"),
                      ("sub_g", "subln_g"), ("g2", "ffn_norm_g"), ("g_mix", "g_mix_2"), ("pool_g", "pool_scale_2"),
                      ("g_xa", "g_xa_2"), ("g_mem", "g_mem_2"), ("g_ffn", "g_ffn_2"), ("g_fin", "g_final_2")):
        put(name, cols(inputs[key]))

    def taps(a):
        a = np.asarray(a)[0]
        return a.reshape(a.shape[0], -1, P).transpose(2, 1, 0).reshape(P, -1)

    put("taps", taps(inputs["conv_dw_w"]))
    put("w_sc", taps(inputs["w_sconv_2"]))
    put("ff_taps", taps(inputs["w_ffconv_2"]))
    for name, keys in (("q_g", ("q_norm_g", "q_norm_g")), ("k_g", ("k_norm_g", "k_norm_g")),
                       ("lam_q", ("lambda_q1", "lambda_q2")), ("lam_k", ("lambda_k1", "lambda_k2"))):
        put(name, np.concatenate([np.asarray(inputs[k])[0] for k in keys]).reshape(P, 1))
    w_r = np.concatenate([np.asarray(inputs["w_router_group"])[0], np.asarray(inputs["w_router_expert"])[0]], 1)
    put("w_r", w_r.reshape(DC, P, 36).transpose(1, 0, 2).reshape(P, -1))
    put("b_r", np.concatenate([np.asarray(inputs["b_router_group"])[0], np.asarray(inputs["b_router_expert"])[0]]).reshape(1, 36), 1)
    put("b_f", np.asarray(inputs["b_forget_2"]).reshape(4, 1), 4)
    w = np.asarray(inputs["w_pool_2"])[0]
    i, _ = at["w_pool"]
    for g in range(4):
        h = 64 * (g % 2)
        par[h:h + 64, i + P * (g // 2) + h:i + P * (g // 2) + h + 64] = w[g]
    return par


def kernel(**inputs):
    import concourse.bacc as bacc
    from concourse.bass_utils import run_bass_kernel_spmd

    nc = bacc.Bacc("TRN2", target_bir_lowering=False, num_devices=1)
    const, places = constants()
    arrays = {"const": const, "par": lay_out(inputs)}
    for name in WEIGHTS:
        arrays[name] = np.ascontiguousarray(inputs[name])
    A = {name: nc.dram_tensor(f"in_{name}_dram", a.shape, mybir.dt.from_np(a.dtype), kind="ExternalInput").ap()
         for name, a in arrays.items()}
    out = nc.dram_tensor("out_0_dram", (1, T, D), F32, kind="ExternalOutput").ap()
    two_blocks_kernel(nc, A, out, places)
    r = run_bass_kernel_spmd(nc, [{f"in_{name}_dram": a for name, a in arrays.items()}], core_ids=[0])
    return r.results[0]["out_0_dram"]
```
